# Optimizing a Trainium2 kernel written in Bass

```python
import math
import jax, jax.numpy as jnp
from jax import lax
import numpy as np

D_MODEL = 1024
BATCH = 1
SEQ = 256
DEPTH = 2

HEAD_DIM = 64
D_MIX = D_MODEL
HA = (D_MIX // 2) // (2 * HEAD_DIM)
HB = (D_MIX // 4) // HEAD_DIM
HC = (D_MIX // 4) // HEAD_DIM
WA = HA * 2 * HEAD_DIM
WB = HB * HEAD_DIM
WC = HC * HEAD_DIM
ROT_DIM = HEAD_DIM // 4
ROPE_THETA = 500000.0
Q_BLOCK = 128
LN_EPS = 1e-5
SUBLN_EPS = 1e-5
DEEPNORM_ALPHA = (2 * DEPTH) ** 0.25
DEEPNORM_BETA = (8 * DEPTH) ** -0.25
SPLIT_SIZES = (WA, WA, WA, WA, WB, WB, WB, HB, WB, WC, WC, WC, WC)
VALUE_SEGMENTS = (2, 6, 11)
D_IN = sum(SPLIT_SIZES)
SPLIT_POINTS = tuple(int(v) for v in np.cumsum(SPLIT_SIZES)[:-1])


def _layernorm(t, g, b):
    tf = t.astype(jnp.float32)
    mu = jnp.mean(tf, -1, keepdims=True)
    var = jnp.mean(jnp.square(tf - mu), -1, keepdims=True)
    out = (tf - mu) * lax.rsqrt(var + LN_EPS) * g.astype(jnp.float32) + b.astype(jnp.float32)
    return out.astype(t.dtype)

def _rope_tables(seq):
    inv = ROPE_THETA ** (-jnp.arange(0, ROT_DIM, 2, dtype=jnp.float32) / ROT_DIM)
    ang = jnp.arange(seq, dtype=jnp.float32)[:, None] * inv[None, :]
    return jnp.cos(ang), jnp.sin(ang)

def _partial_rope(t, cos, sin):
    half = ROT_DIM // 2
    x1 = t[..., :half].astype(jnp.float32)
    x2 = t[..., half:ROT_DIM].astype(jnp.float32)
    r1 = (x1 * cos - x2 * sin).astype(t.dtype)
    r2 = (x2 * cos + x1 * sin).astype(t.dtype)
    return jnp.concatenate([r1, r2, t[..., ROT_DIM:]], axis=-1)

def _split_heads(t, n_heads):
    b_, s_, w_ = t.shape
    return t.reshape(b_, s_, n_heads, w_ // n_heads).transpose(0, 2, 1, 3)

def _to_blocks(t):
    b_, h_, s_ = t.shape[:3]
    t = t.reshape((b_, h_, s_ // Q_BLOCK, Q_BLOCK) + t.shape[3:])
    return jnp.moveaxis(t, 2, 0)

def _from_blocks(t):
    nb, b_, h_, blk, dv = t.shape
    return t.transpose(1, 0, 3, 2, 4).reshape(b_, nb * blk, h_ * dv)

def _differential_attention(q1, q2, k1, k2, v, lam):
    seq = k1.shape[2]
    kpos = jnp.arange(seq)
    starts = jnp.arange(seq // Q_BLOCK) * Q_BLOCK
    scale = HEAD_DIM ** -0.5

    def block(args):
        q1b, q2b, start = args
        qpos = start + jnp.arange(Q_BLOCK)
        causal = kpos[None, :] <= qpos[:, None]
        s1 = jnp.einsum('bhqd,bhkd->bhqk', q1b, k1).astype(jnp.float32) * scale
        s2 = jnp.einsum('bhqd,bhkd->bhqk', q2b, k2).astype(jnp.float32) * scale
        p1 = jax.nn.softmax(jnp.where(causal, s1, -jnp.inf), axis=-1)
        p2 = jax.nn.softmax(jnp.where(causal, s2, -jnp.inf), axis=-1)
        w = (p1 - lam * p2).astype(v.dtype)
        return jnp.einsum('bhqk,bhkd->bhqd', w, v)

    return lax.map(block, (_to_blocks(q1), _to_blocks(q2), starts))

def _forgetting_attention(q, k, v, cum_logf):
    seq = k.shape[2]
    kpos = jnp.arange(seq)
    starts = jnp.arange(seq // Q_BLOCK) * Q_BLOCK
    scale = HEAD_DIM ** -0.5

    def block(args):
        qb, cqb, start = args
        qpos = start + jnp.arange(Q_BLOCK)
        causal = kpos[None, :] <= qpos[:, None]
        s = jnp.einsum('bhqd,bhkd->bhqk', qb, k).astype(jnp.float32) * scale
        logits = s + cqb[..., :, None] - cum_logf[..., None, :]
        p = jax.nn.softmax(jnp.where(causal, logits, -jnp.inf), axis=-1)
        return jnp.einsum('bhqk,bhkd->bhqd', p.astype(v.dtype), v)

    return lax.map(block, (_to_blocks(q), _to_blocks(cum_logf), starts))

def _stick_breaking_attention(q, k, v):
    seq = k.shape[2]
    kpos = jnp.arange(seq)
    starts = jnp.arange(seq // Q_BLOCK) * Q_BLOCK
    scale = HEAD_DIM ** -0.5

    def block(args):
        qb, start = args
        qpos = start + jnp.arange(Q_BLOCK)
        strict = kpos[None, :] < qpos[:, None]
        z = jnp.einsum('bhqd,bhkd->bhqk', qb, k).astype(jnp.float32) * scale
        log_fail = jnp.where(strict, jax.nn.log_sigmoid(-z), 0.0)
        after = lax.cumsum(log_fail, axis=3, reverse=True) - log_fail
        weights = jnp.where(strict, jnp.exp(jax.nn.log_sigmoid(z) + after), 0.0)
        return jnp.einsum('bhqk,bhkd->bhqd', weights.astype(v.dtype), v)

    return lax.map(block, (_to_blocks(q), starts))

def first_inputs(seed: int = 0) -> dict:
    key = jax.random.key(seed)
    ks = jax.random.split(key, 13)
    x = jax.random.normal(ks[0], (BATCH, SEQ, D_MODEL), jnp.float32)
    ln_in_g = 1.0 + 0.02 * jax.random.normal(ks[1], (D_MODEL,), jnp.float32)
    ln_in_b = 0.02 * jax.random.normal(ks[2], (D_MODEL,), jnp.float32)
    col_scale = jnp.concatenate([
        jnp.full((n,), DEEPNORM_BETA if i in VALUE_SEGMENTS else 1.0, jnp.float32)
        for i, n in enumerate(SPLIT_SIZES)])
    w_in = (jax.random.normal(ks[3], (DEPTH, D_MODEL, D_IN), jnp.float32)
            * (D_MODEL ** -0.5) * col_scale)
    b_forget = 1.0 + 0.1 * jax.random.normal(ks[4], (DEPTH, HB), jnp.float32)
    lambda_q1 = 0.1 * jax.random.normal(ks[5], (DEPTH, HEAD_DIM), jnp.float32)
    lambda_k1 = 0.1 * jax.random.normal(ks[6], (DEPTH, HEAD_DIM), jnp.float32)
    lambda_q2 = 0.1 * jax.random.normal(ks[7], (DEPTH, HEAD_DIM), jnp.float32)
    lambda_k2 = 0.1 * jax.random.normal(ks[8], (DEPTH, HEAD_DIM), jnp.float32)
    subln_g = 1.0 + 0.02 * jax.random.normal(ks[9], (DEPTH, 2 * HEAD_DIM), jnp.float32)
    w_out = (jax.random.normal(ks[10], (DEPTH, D_MIX, D_MODEL), jnp.float32)
             * (D_MIX ** -0.5) * DEEPNORM_BETA)
    ln_g = 1.0 + 0.02 * jax.random.normal(ks[11], (DEPTH, D_MODEL), jnp.float32)
    ln_b = 0.02 * jax.random.normal(ks[12], (DEPTH, D_MODEL), jnp.float32)
    return {'x': x, 'ln_in_g': ln_in_g, 'ln_in_b': ln_in_b, 'w_in': w_in,
            'b_forget': b_forget, 'lambda_q1': lambda_q1, 'lambda_k1': lambda_k1,
            'lambda_q2': lambda_q2, 'lambda_k2': lambda_k2, 'subln_g': subln_g,
            'w_out': w_out, 'ln_g': ln_g, 'ln_b': ln_b}

def first_block(x, ln_in_g, ln_in_b, w_in, b_forget, lambda_q1, lambda_k1, lambda_q2,
              lambda_k2, subln_g, w_out, ln_g, ln_b):
    bsz, seq, _ = x.shape
    cos, sin = _rope_tables(seq)
    h = _layernorm(x, ln_in_g, ln_in_b)
    for layer in range(DEPTH):
        proj = jnp.einsum('bsd,de->bse', h, w_in[layer])
        (aq, ak, av, ag, bq, bk, bv, bf, bg, cq, ck, cv, cg) = jnp.split(proj, SPLIT_POINTS, axis=-1)

        qa = _partial_rope(_split_heads(aq, 2 * HA), cos, sin).reshape(bsz, HA, 2, seq, HEAD_DIM)
        ka = _partial_rope(_split_heads(ak, 2 * HA), cos, sin).reshape(bsz, HA, 2, seq, HEAD_DIM)
        va = _split_heads(av, HA)
        lam_init = 0.8 - 0.6 * math.exp(-0.3 * layer)
        lam = (jnp.exp(jnp.sum(lambda_q1[layer].astype(jnp.float32) * lambda_k1[layer].astype(jnp.float32)))
               - jnp.exp(jnp.sum(lambda_q2[layer].astype(jnp.float32) * lambda_k2[layer].astype(jnp.float32)))
               + lam_init)
        oa = _differential_attention(qa[:, :, 0], qa[:, :, 1], ka[:, :, 0], ka[:, :, 1], va, lam)
        oaf = oa.astype(jnp.float32)
        oa = (oaf * lax.rsqrt(jnp.mean(jnp.square(oaf), -1, keepdims=True) + SUBLN_EPS)
              * subln_g[layer].astype(jnp.float32) * (1.0 - lam_init)).astype(h.dtype)
        ya = _from_blocks(oa) * jax.nn.silu(ag)

        logf = jax.nn.log_sigmoid((bf + b_forget[layer]).astype(jnp.float32))
        cum_logf = jnp.cumsum(logf, axis=1).transpose(0, 2, 1)
        ob = _forgetting_attention(_split_heads(bq, HB), _split_heads(bk, HB),
                                   _split_heads(bv, HB), cum_logf)
        yb = _from_blocks(ob) * jax.nn.silu(bg)

        oc = _stick_breaking_attention(_split_heads(cq, HC), _split_heads(ck, HC), _split_heads(cv, HC))
        yc = _from_blocks(oc) * jax.nn.silu(cg)

        y = jnp.einsum('bse,ed->bsd', jnp.concatenate([ya, yb, yc], axis=-1), w_out[layer])
        h = _layernorm(DEEPNORM_ALPHA * h + y, ln_g[layer], ln_b[layer])
    return h


DEPTH_2 = 1

ATTN_HEADS = 8
ATTN_HEAD_DIM = 64
ATTN_WIDTH = ATTN_HEADS * ATTN_HEAD_DIM
KV_RANK = 256
IDX_HEADS = 8
IDX_DIM = 64
TOPK_MAX = 256
ATTN_QBLOCK = 64
N_BUCKETS = 32
MAX_DISTANCE = 128
SSM_HEADS = 16
SSM_HEAD_DIM = 64
SSM_INNER = SSM_HEADS * SSM_HEAD_DIM
SSM_GROUPS = 2
SSM_STATE = 128
CONV_WIDTH = 4
CONV_CH = SSM_INNER + 2 * SSM_GROUPS * SSM_STATE
SSD_CHUNK = 128
N_EXPERTS = 32
TOP_K = 4
D_EXPERT = D_MODEL
SWIGLU_LIMIT = 7.0
SWIGLU_ALPHA = 1.702
MOE_BLOCK = 128
EPS = 1e-6

SPLIT_SIZES_2 = (ATTN_WIDTH, KV_RANK, IDX_HEADS * IDX_DIM, IDX_DIM, IDX_HEADS, SSM_INNER, CONV_CH, SSM_HEADS, 2 * D_MODEL)
D_IN_2 = sum(SPLIT_SIZES_2)


def _rms(x, g, eps=EPS):
    xf = x.astype(jnp.float32)
    y = xf * lax.rsqrt(jnp.mean(xf * xf, axis=-1, keepdims=True) + eps)
    return (y * g.astype(jnp.float32)).astype(x.dtype)

def _layernorm_2(x, g, b, eps=EPS):
    xf = x.astype(jnp.float32)
    mu = jnp.mean(xf, axis=-1, keepdims=True)
    var = jnp.mean(jnp.square(xf - mu), axis=-1, keepdims=True)
    y = (xf - mu) * lax.rsqrt(var + eps) * g.astype(jnp.float32) + b.astype(jnp.float32)
    return y.astype(x.dtype)

def _t5_bucket(dist):
    n = jnp.maximum(dist, 0)
    max_exact = N_BUCKETS // 2
    nf = jnp.maximum(n, 1).astype(jnp.float32)
    large = max_exact + (jnp.log(nf / max_exact) / math.log(MAX_DISTANCE / max_exact) * (N_BUCKETS - max_exact)).astype(jnp.int32)
    large = jnp.minimum(large, N_BUCKETS - 1)
    return jnp.where(n < max_exact, n, large)

def _split(proj):
    idx = [int(i) for i in np.cumsum(SPLIT_SIZES_2)[:-1]]
    return jnp.split(proj, idx, axis=-1)

def _dsa_attention(q, k, v, q_idx, w_idx, k_idx, rel_bias):
    Bsz, L = q.shape[0], q.shape[1]
    topk = min(TOPK_MAX, L // 4)
    nblk = L // ATTN_QBLOCK
    scale = ATTN_HEAD_DIM ** -0.5
    key_pos = jnp.arange(L, dtype=jnp.int32)

    def to_blocks(a):
        return jnp.moveaxis(a.reshape(Bsz, nblk, ATTN_QBLOCK, *a.shape[2:]), 1, 0)

    def block(args):
        qb, qib, wib, start = args
        t = start + jnp.arange(ATTN_QBLOCK, dtype=jnp.int32)
        dots = jnp.einsum('bqhd,bsd->bqhs', qib, k_idx)
        score = jnp.einsum('bqh,bqhs->bqs', wib, jax.nn.relu(dots)).astype(jnp.float32)
        causal = key_pos[None, :] <= t[:, None]
        score = jnp.where(causal[None], score, -jnp.inf)
        _, sel = lax.top_k(score, topk)
        kg = jax.vmap(lambda kk, ii: kk[ii])(k, sel)
        vg = jax.vmap(lambda vv, ii: vv[ii])(v, sel)
        dist = t[None, :, None] - sel
        bias = jnp.moveaxis(rel_bias[_t5_bucket(dist)], -1, 2).astype(jnp.float32)
        logits = jnp.einsum('bqhd,bqkhd->bqhk', qb, kg).astype(jnp.float32) * scale + bias
        logits = jnp.where((dist >= 0)[:, :, None, :], logits, -jnp.inf)
        p = jax.nn.softmax(logits, axis=-1).astype(vg.dtype)
        return jnp.einsum('bqhk,bqkhd->bqhd', p, vg)

    starts = jnp.arange(nblk, dtype=jnp.int32) * ATTN_QBLOCK
    out = lax.map(block, (to_blocks(q), to_blocks(q_idx), to_blocks(w_idx), starts))
    return jnp.moveaxis(out, 0, 1).reshape(Bsz, L, ATTN_WIDTH)

def _mamba2_ssd(z, xbc, dt_raw, conv_w, conv_b, dt_bias, a_log, d_skip, norm_w):
    Bsz, L = xbc.shape[0], xbc.shape[1]
    nc = L // SSD_CHUNK
    hg = SSM_HEADS // SSM_GROUPS
    xbc = lax.conv_general_dilated(xbc, conv_w[:, None, :].astype(xbc.dtype), window_strides=(1,),
                                   padding=[(CONV_WIDTH - 1, 0)], dimension_numbers=('NWC', 'WIO', 'NWC'),
                                   feature_group_count=CONV_CH) + conv_b
    xbc = jax.nn.silu(xbc).astype(jnp.float32)
    xs, bm, cm = jnp.split(xbc, [SSM_INNER, SSM_INNER + SSM_GROUPS * SSM_STATE], axis=-1)
    dt = jax.nn.softplus(dt_raw.astype(jnp.float32) + dt_bias.astype(jnp.float32))
    a = -jnp.exp(a_log.astype(jnp.float32)).reshape(SSM_GROUPS, hg)

    def chunks(arr, *tail):
        return jnp.moveaxis(arr.reshape(Bsz, nc, SSD_CHUNK, *tail), 1, 0)

    x_c = chunks(xs, SSM_GROUPS, hg, SSM_HEAD_DIM)
    dt_c = chunks(dt, SSM_GROUPS, hg)
    b_c = chunks(bm, SSM_GROUPS, SSM_STATE)
    c_c = chunks(cm, SSM_GROUPS, SSM_STATE)
    causal = jnp.tril(jnp.ones((SSD_CHUNK, SSD_CHUNK), dtype=bool))[None, :, :, None, None]

    def step(state, inp):
        xc, dtc, bc, cc = inp
        acum = jnp.cumsum(dtc * a, axis=1)
        seg = acum[:, :, None] - acum[:, None, :]
        lmat = jnp.exp(jnp.where(causal, seg, -jnp.inf))
        cb = jnp.einsum('bign,bjgn->bijg', cc, bc)
        wmat = cb[..., None] * lmat * dtc[:, None]
        y = jnp.einsum('bijgh,bjghp->bighp', wmat, xc)
        y = y + jnp.einsum('bign,bghpn->bighp', cc, state) * jnp.exp(acum)[..., None]
        decay = jnp.exp(acum[:, -1:] - acum) * dtc
        state = state * jnp.exp(acum[:, -1])[..., None, None] + jnp.einsum('bjgn,bjgh,bjghp->bghpn', bc, decay, xc)
        return state, y

    h0 = jnp.zeros((Bsz, SSM_GROUPS, hg, SSM_HEAD_DIM, SSM_STATE), jnp.float32)
    _, ys = lax.scan(step, h0, (x_c, dt_c, b_c, c_c))
    y = jnp.moveaxis(ys, 0, 1).reshape(Bsz, L, SSM_HEADS, SSM_HEAD_DIM)
    y = y + d_skip.astype(jnp.float32)[:, None] * xs.reshape(Bsz, L, SSM_HEADS, SSM_HEAD_DIM)
    y = y.reshape(Bsz, L, SSM_INNER) * jax.nn.silu(z.astype(jnp.float32))
    yg = y.reshape(Bsz, L, SSM_GROUPS, SSM_INNER // SSM_GROUPS)
    yg = yg * lax.rsqrt(jnp.mean(yg * yg, axis=-1, keepdims=True) + EPS)
    y = yg.reshape(Bsz, L, SSM_INNER) * norm_w.astype(jnp.float32)
    return y.astype(z.dtype)

def _moe(h, w_router, b_router, w_gu, b_gu, w_dn, b_dn):
    Bsz, L, D = h.shape
    T = Bsz * L
    hf = h.reshape(T, D)
    logits = (hf @ w_router + b_router).astype(jnp.float32)
    top_val, top_idx = lax.top_k(logits, TOP_K)
    gates = jax.nn.softmax(top_val, axis=-1)
    n_assign = T * TOP_K
    e_flat = top_idx.reshape(n_assign)
    g_flat = gates.reshape(n_assign)
    tok_flat = jnp.arange(n_assign, dtype=jnp.int32) // TOP_K
    order = jnp.argsort(e_flat)
    e_sorted = e_flat[order]
    counts = jnp.bincount(e_flat, length=N_EXPERTS)
    padded = (counts + MOE_BLOCK - 1) // MOE_BLOCK * MOE_BLOCK
    pad_end = jnp.cumsum(padded)
    pad_start = pad_end - padded
    start = jnp.cumsum(counts) - counts
    rank = jnp.arange(n_assign, dtype=jnp.int32) - start[e_sorted]
    dest = pad_start[e_sorted] + rank
    n_rows = n_assign + N_EXPERTS * MOE_BLOCK
    row_tok = jnp.full((n_rows,), T, dtype=jnp.int32).at[dest].set(tok_flat[order])
    row_gate = jnp.zeros((n_rows,), jnp.float32).at[dest].set(g_flat[order])
    n_blk = n_rows // MOE_BLOCK
    blk_start = jnp.arange(n_blk, dtype=jnp.int32) * MOE_BLOCK
    blk_exp = jnp.minimum(jnp.sum(blk_start[:, None] >= pad_end[None, :], axis=1), N_EXPERTS - 1)
    h_pad = jnp.concatenate([hf, jnp.zeros((1, D), hf.dtype)], axis=0)

    def run_block(args):
        toks, e = args
        xb = h_pad[toks]
        gu = xb @ w_gu[e] + b_gu[e]
        g, u = gu[:, :D_EXPERT], gu[:, D_EXPERT:]
        g = jnp.minimum(g, SWIGLU_LIMIT)
        u = jnp.clip(u, -SWIGLU_LIMIT, SWIGLU_LIMIT)
        act = (u + 1.0) * (g * jax.nn.sigmoid(SWIGLU_ALPHA * g))
        return act @ w_dn[e] + b_dn[e]

    out = lax.map(run_block, (row_tok.reshape(n_blk, MOE_BLOCK), blk_exp))
    out = out.reshape(n_rows, D) * row_gate[:, None].astype(out.dtype)
    y = jax.ops.segment_sum(out, row_tok, num_segments=T + 1)[:T]
    return y.reshape(Bsz, L, D)

def second_inputs(seed: int = 0) -> dict:
    key = jax.random.key(seed)
    ks = jax.random.split(key, 32)
    f32 = jnp.float32

    def nrm(k, shape, scale):
        return jax.random.normal(k, shape, f32) * scale

    def gain(k, shape):
        return 1.0 + 0.05 * jax.random.normal(k, shape, f32)

    dt = jnp.exp(jax.random.uniform(ks[17], (DEPTH_2, SSM_HEADS), f32, math.log(1e-3), math.log(1e-1)))
    return {
        'x': nrm(ks[0], (BATCH, SEQ, D_MODEL), 1.0),
        'c': nrm(ks[1], (BATCH, D_MODEL), 1.0),
        'rel_bias': nrm(ks[2], (N_BUCKETS, ATTN_HEADS), 0.5),
        'w_ada': nrm(ks[3], (DEPTH_2, D_MODEL, 6 * D_MODEL), 0.5 * D_MODEL ** -0.5),
        'b_ada': nrm(ks[4], (DEPTH_2, 6 * D_MODEL), 0.02),
        'norm_mix': gain(ks[5], (DEPTH_2, D_MODEL)),
        'norm_ffn': gain(ks[6], (DEPTH_2, D_MODEL)),
        'w_in': nrm(ks[7], (DEPTH_2, D_MODEL, D_IN_2), D_MODEL ** -0.5),
        'kv_norm': gain(ks[8], (DEPTH_2, KV_RANK)),
        'w_kv_up': nrm(ks[9], (DEPTH_2, KV_RANK, 2 * ATTN_WIDTH), KV_RANK ** -0.5),
        'q_norm': gain(ks[10], (DEPTH_2, ATTN_HEAD_DIM)),
        'k_norm': gain(ks[11], (DEPTH_2, ATTN_HEAD_DIM)),
        'idx_k_ln_w': gain(ks[12], (DEPTH_2, IDX_DIM)),
        'idx_k_ln_b': nrm(ks[13], (DEPTH_2, IDX_DIM), 0.02),
        'w_attn_o': nrm(ks[14], (DEPTH_2, ATTN_WIDTH, D_MODEL), ATTN_WIDTH ** -0.5),
        'conv_w': nrm(ks[15], (DEPTH_2, CONV_WIDTH, CONV_CH), CONV_WIDTH ** -0.5),
        'conv_b': nrm(ks[16], (DEPTH_2, CONV_CH), 0.02),
        'dt_bias': dt + jnp.log(-jnp.expm1(-dt)),
        'a_log': jnp.log(jax.random.uniform(ks[18], (DEPTH_2, SSM_HEADS), f32, 1.0, 16.0)),
        'd_skip': gain(ks[19], (DEPTH_2, SSM_HEADS)),
        'ssm_norm': gain(ks[20], (DEPTH_2, SSM_INNER)),
        'w_ssm_o': nrm(ks[21], (DEPTH_2, SSM_INNER, D_MODEL), SSM_INNER ** -0.5),
        'w_out': nrm(ks[22], (DEPTH_2, D_MODEL, D_MODEL), D_MODEL ** -0.5),
        'w_router': nrm(ks[23], (DEPTH_2, D_MODEL, N_EXPERTS), D_MODEL ** -0.5),
        'b_router': nrm(ks[24], (DEPTH_2, N_EXPERTS), 0.01),
        'w_gu': nrm(ks[25], (DEPTH_2, N_EXPERTS, D_MODEL, 2 * D_EXPERT), D_MODEL ** -0.5),
        'b_gu': nrm(ks[26], (DEPTH_2, N_EXPERTS, 2 * D_EXPERT), 0.02),
        'w_dn': nrm(ks[27], (DEPTH_2, N_EXPERTS, D_EXPERT, D_MODEL), D_EXPERT ** -0.5),
        'b_dn': nrm(ks[28], (DEPTH_2, N_EXPERTS, D_MODEL), 0.02),
    }

def second_block(x, c, rel_bias, w_ada, b_ada, norm_mix, norm_ffn, w_in, kv_norm, w_kv_up, q_norm, k_norm,
              idx_k_ln_w, idx_k_ln_b, w_attn_o, conv_w, conv_b, dt_bias, a_log, d_skip, ssm_norm, w_ssm_o,
              w_out, w_router, b_router, w_gu, b_gu, w_dn, b_dn):
    Bsz, L, _ = x.shape
    cond = jax.nn.silu(c)
    for l in range(DEPTH_2):
        mod = cond @ w_ada[l] + b_ada[l]
        sh_m, sc_m, g_m, sh_f, sc_f, g_f = jnp.split(mod[:, None, :], 6, axis=-1)
        h = _rms(x, norm_mix[l]) * (1.0 + sc_m) + sh_m
        proj = h @ w_in[l]
        q, kv_lat, q_i, k_i, w_i, z, xbc, dt_raw, gate_logits = _split(proj)
        q = _rms(q.reshape(Bsz, L, ATTN_HEADS, ATTN_HEAD_DIM), q_norm[l])
        kv = _rms(kv_lat, kv_norm[l]) @ w_kv_up[l]
        k, v = jnp.split(kv, 2, axis=-1)
        k = _rms(k.reshape(Bsz, L, ATTN_HEADS, ATTN_HEAD_DIM), k_norm[l])
        v = v.reshape(Bsz, L, ATTN_HEADS, ATTN_HEAD_DIM)
        q_i = q_i.reshape(Bsz, L, IDX_HEADS, IDX_DIM) * (IDX_DIM ** -0.5)
        w_i = w_i * (IDX_HEADS ** -0.5)
        k_i = _layernorm_2(k_i, idx_k_ln_w[l], idx_k_ln_b[l])
        y_attn = _dsa_attention(q, k, v, q_i, w_i, k_i, rel_bias) @ w_attn_o[l]
        y_ssd = _mamba2_ssd(z, xbc, dt_raw, conv_w[l], conv_b[l], dt_bias[l], a_log[l], d_skip[l], ssm_norm[l]) @ w_ssm_o[l]
        g_attn, g_ssd = jnp.split(gate_logits, 2, axis=-1)
        mixed = jax.nn.sigmoid(g_attn) * y_attn + jax.nn.sigmoid(g_ssd) * y_ssd
        x = x + g_m * (mixed @ w_out[l])
        h = _rms(x, norm_ffn[l]) * (1.0 + sc_f) + sh_f
        x = x + g_f * _moe(h, w_router[l], b_router[l], w_gu[l], b_gu[l], w_dn[l], b_dn[l])
    return x


def setup_inputs(seed=0):
    out = dict(first_inputs(seed))
    for name, value in second_inputs(seed + 1).items():
        if name != "x":
            out[name + "_2"] = value
    return out


def reference(
    x, ln_in_g, ln_in_b, w_in, b_forget, lambda_q1, lambda_k1, lambda_q2, lambda_k2, subln_g,
    w_out, ln_g, ln_b, c_2, rel_bias_2, w_ada_2, b_ada_2, norm_mix_2, norm_ffn_2, w_in_2,
    kv_norm_2, w_kv_up_2, q_norm_2, k_norm_2, idx_k_ln_w_2, idx_k_ln_b_2, w_attn_o_2, conv_w_2,
    conv_b_2, dt_bias_2, a_log_2, d_skip_2, ssm_norm_2, w_ssm_o_2, w_out_2, w_router_2,
    b_router_2, w_gu_2, b_gu_2, w_dn_2, b_dn_2,
):
    x = first_block(
        x, ln_in_g, ln_in_b, w_in, b_forget, lambda_q1, lambda_k1, lambda_q2, lambda_k2,
        subln_g, w_out, ln_g, ln_b,
    )
    return second_block(
        x, c_2, rel_bias_2, w_ada_2, b_ada_2, norm_mix_2, norm_ffn_2, w_in_2, kv_norm_2,
        w_kv_up_2, q_norm_2, k_norm_2, idx_k_ln_w_2, idx_k_ln_b_2, w_attn_o_2, conv_w_2,
        conv_b_2, dt_bias_2, a_log_2, d_skip_2, ssm_norm_2, w_ssm_o_2, w_out_2, w_router_2,
        b_router_2, w_gu_2, b_gu_2, w_dn_2, b_dn_2,
    )


_drawn_inputs = setup_inputs


def setup_inputs(seed=0):
    import zlib

    import numpy as np

    out = dict(_drawn_inputs(seed))
    spreads = {}
    factors = {'b_forget': 34.08,
     'lambda_q1': 3.931,
     'lambda_q2': 2.789,
     'lambda_k2': 3.61,
     'subln_g': 8.0,
     'rel_bias_2': 2.773,
     'norm_mix_2': 3.179,
     'kv_norm_2': 8.0,
     'q_norm_2': 8.0,
     'k_norm_2': 8.0,
     'idx_k_ln_w_2': 6.594,
     'idx_k_ln_b_2': 8.0,
     'conv_b_2': 8.0,
     'd_skip_2': 176.645,
     'ssm_norm_2': 5.919,
     'b_router_2': 20.597,
     'b_gu_2': 31.398,
     'b_dn_2': 37.069,
     'norm_ffn_2': 3.932}
    for name, (base, spread) in spreads.items():
        noise = np.random.default_rng([zlib.crc32(name.encode()), seed]).standard_normal(out[name].shape)
        drawn = base * np.exp(spread * noise) if base else spread * noise
        out[name] = __import__('jax').numpy.asarray(drawn.astype(out[name].dtype))
    for name, factor in factors.items():
        out[name] = (out[name] * factor).astype(out[name].dtype)
    return out
```

```python
import math
from contextlib import ExitStack

import numpy as np

import concourse.bass as bass
from concourse import mybir

F32 = mybir.dt.float32
I32 = mybir.dt.int32
ALU = mybir.AluOpType
ACT = mybir.ActivationFunctionType
AX_X = mybir.AxisListType.X

P = 128
BIG = 1e30
RING = 4
BANKS = 8
CAP = 64
LN_EPS = 1e-5
RMS_EPS = 1e-6
HEAD = 64


def layer_lambda(layer):
    return 0.8 - 0.6 * math.exp(-0.3 * layer)


def constants(T):
    i = np.arange(P)
    f = np.float32
    up = (i[:, None] <= i[None, :]).astype(f)
    ones = np.ones((P, P), f)
    half = (i[:, None] // HEAD == i[None, :] // HEAD).astype(f)
    rot = np.zeros((P, P), f)
    for h in range(2):
        for j in range(8):
            rot[h * HEAD + 8 + j, h * HEAD + j] = -1.0
            rot[h * HEAD + j, h * HEAD + 8 + j] = 1.0
    inv = f(500000.0) ** (-np.arange(0, 16, 2, dtype=f) / f(16))
    ang = np.arange(T, dtype=f)[:, None] * inv[None, :].astype(f)
    cos = np.ones((P, T), f)
    sin = np.zeros((P, T), f)
    for h in range(2):
        for part in range(2):
            a = h * HEAD + 8 * part
            cos[a:a + 8] = np.cos(ang).T
            sin[a:a + 8] = np.sin(ang).T
    tri = np.where(i[None, :] <= i[:, None], 0.0, -BIG).astype(f)
    row_mask = np.concatenate([tri, np.zeros((P, P), f), tri], 1)
    col = np.where(i[:, None] <= i[None, :], 0.0, -BIG).astype(f)
    col_mask = np.concatenate([col, np.zeros((P, P), f), col], 1)
    strict = (i[:, None] < i[None, :]).astype(f)
    strict_neg = -np.concatenate([strict, ones, strict], 1)
    strict_add = np.where(strict_neg < 0, 0.0, -BIG).astype(f)
    dist = np.maximum(T - 1 - np.arange(2 * T), 0)
    n = np.maximum(dist, 1).astype(f)
    large = 16 + (np.log(n / 16) / math.log(8.0) * 16).astype(np.int32)
    bucket = np.where(dist < 16, dist, np.minimum(large, 31))
    hot = np.zeros((P, 2 * T), f)
    hot[bucket, np.arange(2 * T)] = 1.0
    iota = np.tile(np.arange(CAP, dtype=f), (P, 1))
    return {
        "ident": np.eye(P, dtype=f), "up_ones": np.concatenate([up, ones], 1), "down": up.T.copy(),
        "half": half / HEAD, "rot": rot, "cos": cos, "sin": sin,
        "row_mask": row_mask, "col_mask": col_mask, "strict_neg": strict_neg,
        "strict_add": strict_add, "hot": hot, "iota": iota,
        "before": up - np.eye(P, dtype=f),
    }


def mixer_moe_kernel(nc, a, out):
    T, D = a["x"].shape[1:]
    NB = T // P
    KC = D // P
    DEPTH = a["w_in"].shape[0]
    NE = a["w_gu_2"].shape[1]
    DE = a["w_dn_2"].shape[2]
    assert (T, D, NB, KC, DE) == (256, 1024, 2, 8, 1024)
    HA, HB, HC = 4, 4, 4
    AH, SH = 8, 16
    TOPK, TOPE = 64, 4
    alpha = (2 * DEPTH) ** 0.25
    W3 = 3 * P
    COLS = 528
    MAX_EXTRA = (TOPE * T - 1) // (CAP + 1)

    ctx = ExitStack()

    def sem(name):
        return ctx.enter_context(nc.semaphore(name))

    def sb(name, shape, dt=F32, where=ctx):
        return where.enter_context(nc.sbuf_tensor(name, shape, dt))

    consts = constants(T)
    FIRST_CONSTS = ("hot", "rot", "cos", "sin", "strict_neg", "strict_add")
    const_dram, K = {}, {}
    for name, value in consts.items():
        const_dram[name] = nc.inline_tensor(value, name="c_" + name)
        K[name] = None if name in FIRST_CONSTS else sb("k_" + name, list(value.shape))
    ident, up_ones = K["ident"], K["up_ones"]
    up = up_ones[:, 0:P]
    ones = up_ones[:, P:2 * P]

    rows_of = {}
    row_loads = []
    vec_tiles = [0, 0]

    def add_rows(tile, name, source, n):
        rows_of[name] = (tile, vec_tiles[tile])
        row_loads.append((tile, vec_tiles[tile], n, source))
        vec_tiles[tile] += n

    chunk = lambda v: v.rearrange("(c p) -> c p", p=P)
    add_rows(0, "ln_in_g", chunk(a["ln_in_g"]), 8)
    add_rows(0, "ln_in_b", chunk(a["ln_in_b"]), 8)
    add_rows(0, "ln_g", a["ln_g"].rearrange("l (c p) -> (l c) p", p=P), 8 * DEPTH)
    add_rows(0, "ln_b", a["ln_b"].rearrange("l (c p) -> (l c) p", p=P), 8 * DEPTH)
    add_rows(0, "subln_g", a["subln_g"], DEPTH)
    add_rows(0, "norm_mix", chunk(a["norm_mix_2"][0]), 8)
    add_rows(0, "norm_ffn", chunk(a["norm_ffn_2"][0]), 8)
    add_rows(0, "kv_norm", chunk(a["kv_norm_2"][0]), 2)
    add_rows(0, "conv_w", a["conv_w_2"][0].rearrange("k (c p) -> (k c) p", p=P), 48)
    add_rows(1, "conv_b", chunk(a["conv_b_2"][0]), 12)
    add_rows(1, "ssm_norm", chunk(a["ssm_norm_2"][0]), 8)
    add_rows(1, "c", a["c_2"].rearrange("o (c p) -> (o c) p", p=P), 8)
    add_rows(1, "b_ada", a["b_ada_2"].rearrange("o (c p) -> (o c) p", p=P), 48)
    twice = []
    for name in ("q_norm_2", "k_norm_2", "idx_k_ln_w_2", "idx_k_ln_b_2"):
        rows_of[name] = (1, vec_tiles[1])
        twice.append((vec_tiles[1], a[name]))
        vec_tiles[1] += 1
    vecs = sb("vecs", [P, 2, P])
    bgu = sb("bgu", [P, 4 * P])
    N_BGU = NE * 2 * DE // P // P

    def vec(name, c=0, n=1):
        tile, at = rows_of[name]
        return vecs[:, tile, at + c:at + c + n]

    b_forget = sb("b_forget", [P, DEPTH * HB])
    dt_bias = sb("dt_bias", [P, SH])
    a_log = sb("a_log", [P, SH])
    b_router = sb("b_router", [P, NE])
    d_skip = sb("d_skip", [P, KC])
    rel_bias = sb("rel_bias", [32, AH])
    biasrev = sb("biasrev", [AH, 2 * T])
    means = sb("means", [P, 4, P])
    eps = sb("eps", [P, 2])
    sink = sb("sink", [P, 1])
    w_router = sb("w_router", [P, KC, NE])

    hT = sb("hT", [P, KC, T])
    xT = sb("xT", [P, KC, T])
    wide = sb("wide", [P, KC, T])
    stat = sb("stat", [P, T])
    modT = sb("modT", [P, 48])
    mix_scale = sb("mix_scale", [P, 16])
    condT = sb("condT", [P, KC])
    ring = sb("ring", [P, RING, KC * COLS])

    psum = ctx.enter_context(nc.psum_tensor("psum", [P, BANKS, 512], F32))

    first = ExitStack()
    x_in = sb("x_in", [P, NB, D], where=first)
    for name in FIRST_CONSTS:
        K[name] = sb("k_" + name, list(consts[name].shape), where=first)
    vec_rows = sb("vec_rows", [P, 2, P], where=first)
    bgu_rows = sb("bgu_rows", [P, 4, P], where=first)
    lam_in = sb("lam_in", [P, 4, DEPTH * HEAD], where=first)
    qk_raw = sb("qk_raw", [P, 8, T], where=first)
    qk = sb("qk", [P, 8, T], where=first)
    bc_qk = sb("bc_qk", [P, 8, T], where=first)
    va = sb("va", [P, NB, 512], where=first)
    vbc = sb("vbc", [P, NB, 512], where=first)
    gate = x_in[:, :, :].rearrange("p b d -> p (b d)").rearrange("p (c t) -> p c t", c=KC)
    yT = sb("yT", [P, KC, T], where=first)
    sc = sb("sc", [P, 8, W3], where=first)
    sf = sb("sf", [P, 4, W3], where=first)
    zs = sb("zs", [P, 4, W3], where=first)
    ls = sb("ls", [P, 4, W3], where=first)
    probT = sb("probT", [P, 2, W3], where=first)
    row_max = sb("row_max", [P, 24], where=first)
    row_sum = sb("row_sum", [P, 24], where=first)
    small = sb("small", [P, 64], where=first)
    lam = sb("lam", [P, 8], where=first)
    logf = sb("logf", [P, NB, HB], where=first)
    cumq = sb("cumq", [P, NB * HB], where=first)
    first.close()

    second = ExitStack()
    q2 = sb("q2", [P, 4, T], where=second)
    kvl = sb("kvl", [P, 2, T], where=second)
    qi = sb("qi", [P, 4, T], where=second)
    ki = sb("ki", [P, T], where=second)
    wi = sb("wi", [P, NB, AH], where=second)
    k2 = sb("k2", [P, 4, T], where=second)
    v2 = sb("v2", [P, NB, 512], where=second)
    zg = sb("zg", [P, KC, T], where=second)
    xbc = sb("xbc", [P, 12, T + 3], where=second)
    yS = xbc[:, :, :].rearrange("p c t -> p (c t)")[:, 0:KC * T].rearrange("p (c t) -> p c t", c=KC)
    xbcs = sb("xbcs", [P, 12, T], where=second)
    gs = xbcs[:, 0:KC, :]
    ga = sb("ga", [P, KC, T], where=second)
    sc2 = sb("sc2", [P, 8, W3], where=second)
    early = sc2[:, :, :].rearrange("p h n -> p (h n)")
    x_tok = early[:, 0:NB * D].rearrange("p (b d) -> p b d", b=NB)
    decay = early[:, NB * D:NB * D + 2 * W3].rearrange("p (i n) -> p i n", i=2)
    bm = sb("bm", [P, 8, W3], where=second)
    probT2 = sb("probT2", [P, 2, W3], where=second)
    cbs = sb("cbs", [P, 2, W3], where=second)
    idx = sb("idx", [P, 4, W3], where=second)
    top8 = sb("top8", [P, 2, 8], where=second)
    sm = sb("sm", [P, 16], where=second)
    row_max2 = sb("row_max2", [P, 16], where=second)
    row_sum2 = sb("row_sum2", [P, 16], where=second)
    dtx = sb("dtx", [P, 4, NB * SH], where=second)
    dt = sb("dt", [P, NB, SH], where=second)
    dta = sb("dta", [P, NB, SH], where=second)
    neg_acum = sb("neg_acum", [P, 3, SH], where=second)
    exp_a = sb("exp_a", [P, SH], where=second)
    second.close()

    third = ExitStack()
    h_tok = sb("h_tok", [P, NB, D], where=third)
    w_down = sb("w_down", [P, 2, KC * 512], where=third)
    b_dn = sb("b_dn", [NE, D], where=third)
    hg = sb("hg", [P, KC, CAP], where=third)
    guT = sb("guT", [P, 2, KC, CAP], where=third)
    actT = sb("actT", [P, 3, KC, CAP], where=third)
    o_slot = sb("o_slot", [CAP, D], where=third)
    pick = sb("pick", [P, NB, CAP], where=third)
    pick_gate = sb("pick_gate", [P, NB, CAP], where=third)
    putT = sb("putT", [CAP, T], where=third)
    rt = sb("rt", [P, 8, NB, NE], where=third)
    rsm = sb("rsm", [P, 32], where=third)
    pos = sb("pos", [P, NB, 4, NE], where=third)
    gateT = sb("gateT", [NE, T], where=third)
    passes = sb("passes", [NE, 24], where=third)
    todo_f = sb("todo_f", [1, 2 * MAX_EXTRA + 2], where=third)
    todo = sb("todo", [1, 2 * MAX_EXTRA + 2], I32, where=third)
    zero = sb("zero", [P, P], where=third)
    third.close()

    bias_dram = nc.dram_tensor("bias_scratch", (AH, P, 2 * T), F32)

    slot_full = [sem(f"slot_full{i}") for i in range(RING)]
    bank_full = [sem(f"bank_full{i}") for i in range(BANKS)]
    bank_free = [sem(f"bank_free{i}") for i in range(BANKS)]
    events = {}

    def ev(name):
        if name not in events:
            events[name] = sem("e_" + name)
        return events[name]

    groups = []

    def group(name, w, a0, a1):
        groups.append((name, w.rearrange("(k p) n -> p k n", p=P)[:, :, a0:a1]))

    FIRST_GROUPS = [("q", 0, 512), ("k", 512, 1024), ("va", 1024, 1536), ("ga", 1536, 2048),
                    ("bqk", 2048, 2560), ("bvfg", 2560, 3076), ("cqk", 3076, 3588), ("cvg", 3588, 4100)]
    ADA_AT = {"scores": 3, "last": 3}
    ada_next = [0]

    def ada_groups(n):
        for _ in range(n):
            g = ada_next[0]
            group(f"ada{g}", a["w_ada_2"][0], 512 * g, 512 * g + 512)
            ada_next[0] += 1

    for l in range(DEPTH):
        for name, a0, a1 in FIRST_GROUPS:
            group(f"{name}{l}", a["w_in"][l], a0, a1)
        ada_groups(12 // DEPTH)
        for j in range(2):
            group(f"out{l}.{j}", a["w_out"][l], 512 * j, 512 * j + 512)
    for name, a0, a1 in [("q2", 0, 512), ("kvqi", 512, 1024), ("qkwi", 1024, 1352),
                         ("x0", 2376, 2888), ("x1", 2888, 3400), ("x2", 3400, 3912), ("dtg", 3912, 4440),
                         ("z0", 1352, 1864), ("z1", 1864, 2376),
                         ("g1", 4440, 4952), ("g2", 4952, 5464), ("g3", 5464, 5976)]:
        if name == "g1":
            group("kvup", a["w_kv_up_2"][0], 0, 1024)
        group(name, a["w_in_2"][0], a0, a1)
    group("ao", a["w_attn_o_2"][0], 0, 1024)
    for j in range(2):
        group(f"so{j}", a["w_ssm_o_2"][0], 512 * j, 512 * j + 512)
    for j in range(2):
        group(f"wo{j}", a["w_out_2"][0], 512 * j, 512 * j + 512)
    place = {name: g for g, (name, _) in enumerate(groups)}
    NG = len(groups)

    def slot_view(slot, k, n):
        return ring[:, slot, 0:k * n].rearrange("p (k n) -> p k n", k=k)

    expert_slot = [(NG + j) % RING for j in range(4)]
    slot_uses = [len(range(s, NG, RING)) for s in range(RING)]
    w_gu = a["w_gu_2"][0].rearrange("e (k p) n -> e p k n", p=P)
    w_dn = a["w_dn_2"][0].rearrange("e (k p) n -> e p k n", p=P)

    banks = {}
    slot_last = {}

    def product(eng, name):
        b, n = banks[name]
        eng.wait_ge(bank_full[b], n + 1)
        return psum[:, b, :]

    def read_out(eng, name):
        b, n = banks[name]
        eng.wait_ge(bank_free[b], n + 1)

    values_done = {}

    def flat(v):
        v = v[:, :, :] if len(v.shape) == 3 else v
        return v.rearrange("p a b -> p (a b)")

    def dt2(v):
        return v[:, :, :].rearrange("p b h -> p (b h)")

    def shaped(v, like):
        if len(like.shape) == 3:
            return v.rearrange("p (c t) -> p c t", c=like.shape[1])
        return v

    def row_exp(act, scores, h0, n, maxima, sums, c0, c1, s):
        for h in range(n):
            act.activation(scores[:, h, 0:P], scores[:, h, 0:P], ACT.Exp, bias=maxima[:, c0 + h:c0 + h + 1],
                           accum_out=sums[:, c0 + h:c0 + h + 1])
            ins = act.activation(scores[:, h, P:W3], scores[:, h, P:W3], ACT.Exp,
                                 bias=maxima[:, c1 + h:c1 + h + 1], accum_out=sums[:, c1 + h:c1 + h + 1])
        ins.then_inc(s, 1)

    N_BCAST = 12

    class Chain:

        def __init__(self, eng, name):
            self.eng, self.sem, self.count = eng, sem(name), {}

        def after(self, ins, s=None):
            s = self.sem if s is None else s
            ins.then_inc(s, 1)
            key = str(s)
            self.count[key] = self.count.get(key, 0) + 1
            self.eng.wait_ge(s, self.count[key])

        def free(self, ins, name):
            b, n = banks[name]
            ins.then_inc(bank_free[b], 1)
            self.eng.wait_ge(bank_free[b], n + 1)

    block = ctx.enter_context(nc.Block())

    @block.tensor
    def _(pe):
        def take(name):
            n = len(banks)
            banks[name] = (n % BANKS, n // BANKS)
            if n >= BANKS:
                pe.wait_ge(bank_free[n % BANKS], n // BANKS)
            return psum[:, n % BANKS, :]

        def full(mm, name):
            b, n = banks[name]
            mm.then_inc(bank_full[b], 1)

        def weights(name):
            g = place[name]
            pe.wait_ge(slot_full[g % RING], 16 * (g // RING + 1))
            _, src = groups[g]
            return slot_view(g % RING, src.shape[1], src.shape[2])

        def last_of(group_name, product):
            b, n = banks[product]
            slot_last[place[group_name]] = (bank_full[b], n + 1)

        def features(name, w, src, c0, n, m=P):
            bank = take(name)
            k_n = w.shape[1]
            for c in range(n):
                for k in range(k_n):
                    mm = pe.matmul(bank[0:m, c * T:(c + 1) * T], w[:, k, c0 + c * P:c0 + c * P + m],
                                   src[:, k, :], start=(k == 0), stop=(k == k_n - 1))
            full(mm, name)

        def tokens(name, w, src, blk, c0, n):
            bank = take(name)
            k_n = w.shape[1]
            for k in range(k_n):
                mm = pe.matmul(bank[:, 0:n], src[:, k, blk * P:(blk + 1) * P], w[:, k, c0:c0 + n],
                               start=(k == 0), stop=(k == k_n - 1))
            full(mm, name)

        def sum_chunks(name, src, ks, lhs):
            bank = take(name)
            for n, cs in enumerate(ks):
                for c in cs:
                    mm = pe.matmul(bank[:, n * T:(n + 1) * T], lhs, src[:, c, :],
                                   start=(c == cs[0]), stop=(c == cs[-1]))
            full(mm, name)

        def head_rows(name, q, qc, k, kc, half):
            bank = take(name)
            r = slice(half * HEAD, half * HEAD + HEAD)
            pe.matmul(bank[:, 0:P], q[r, qc, 0:P], k[r, kc, 0:P], start=True, stop=True)
            mm = pe.matmul(bank[:, P:W3], q[r, qc, P:T], k[r, kc, 0:T], start=True, stop=True)
            full(mm, name)

        def turn_rows(name, src):
            bank = take(name)
            for j in range(3):
                mm = pe.transpose(bank[:, j * P:(j + 1) * P], src[:, j * P:(j + 1) * P], ident[:, :])
            full(mm, name)

        def apply_values(bank, c, v, cols, wT, half=None):
            rows = slice(0, P) if half is None else slice(half * HEAD, half * HEAD + HEAD)
            pe.matmul(bank[rows, c * T:(c + 1) * T], v[:, 0, cols], wT[:, 0:T], start=True, stop=False)
            return pe.matmul(bank[rows, c * T + P:(c + 1) * T], v[:, 1, cols], wT[:, T:W3],
                             start=False, stop=True)

        def norm_sums(tag, src, centred):
            if centred:
                read_out(pe, centred)
                sum_chunks(tag + "mean", src, [range(KC)], ones_d)
            pe.wait_ge(ev("sq_d"), norm_sums.n + 1)
            norm_sums.n += 1
            sum_chunks(tag + "var", wide, [range(KC)], ones_d)
        norm_sums.n = 0
        ones_d = means[:, 0, :]

        def head_values(tag, heads, turned_rows, v, v_cols, prob, first_i, product_of, where):
            for i in range(heads + 1):
                if i < heads:
                    turned_rows(i)
                if i >= 1:
                    h = i - 1
                    name = product_of(h)
                    if name not in banks:
                        take(name)
                    read_out(pe, f"{tag}t{h}")
                    c, half = where(h)
                    mm = apply_values(psum[:, banks[name][0], :], c, v, v_cols(h), prob[:, (first_i + h) % 2, :], half)
                    if h == heads - 1 or product_of(h + 1) != name:
                        full(mm, name)
                        b, n = banks[name]
                        values_done[(tag, h)] = (bank_full[b], n + 1)
                    else:
                        mm.then_inc(ev("values"), 1)
                        head_values.n += 1
                        values_done[(tag, h)] = (ev("values"), head_values.n)
        head_values.n = 0

        def ssm_values(h):
            pe.wait_ge(ev("decay"), h + 1)
            name = f"yssm{h // 4}"
            if h % 4 == 0:
                take(name)
            mm = apply_values(psum[:, banks[name][0], :], h // 2 % 2, x_tok, slice(h * HEAD, (h + 1) * HEAD),
                              decay[:, h % 2, :], h % 2)
            if h % 4 == 3:
                full(mm, name)
                b, n = banks[name]
                values_done[("ssm", h)] = (bank_full[b], n + 1)
            else:
                mm.then_inc(ev("values"), 1)
                head_values.n += 1
                values_done[("ssm", h)] = (ev("values"), head_values.n)

        pe.wait_ge(ev("const_in"), 16 * len(consts))
        pe.wait_ge(ev("rows_in"), 16 * (len(row_loads) + 2 * len(twice)))
        pe.wait_ge(ev("means_set"), 6)
        bank = take("vecs")
        for t in range(2):
            mm = pe.transpose(bank[:, t * P:t * P + vec_tiles[t]], vec_rows[0:vec_tiles[t], t, :],
                              ident[0:vec_tiles[t], 0:vec_tiles[t]])
        full(mm, "vecs")
        pe.wait_ge(ev("bgu_in"), 16)
        bank = take("bgu")
        for t in range(N_BGU):
            mm = pe.transpose(bank[:, t * P:(t + 1) * P], bgu_rows[:, t, :], ident[:, :])
        full(mm, "bgu")
        pe.wait_ge(ev("x_in"), 16)
        for c in range(0, KC, 2):
            bank = take(f"x{c}")
            for j in range(2):
                for b in range(NB):
                    mm = pe.transpose(bank[:, (j * NB + b) * P:(j * NB + b + 1) * P],
                                      x_in[:, b, (c + j) * P:(c + j + 1) * P], ident[:, :])
            full(mm, f"x{c}")
        bank = take("bias")
        pe.wait_ge(ev("bcast_in"), 16 * N_BCAST)
        mm = pe.matmul(bank[0:AH, :], rel_bias[:, :], K["hot"][0:32, :], start=True, stop=True)
        full(mm, "bias")
        norm_sums("in.", xT, "x6")

        def ada(n):
            for g in range(ada.g, ada.g + n):
                if g == 0:
                    pe.wait_ge(ev("cond"), 1)
                w = weights(f"ada{g}")
                bank = take(f"ada{g}")
                for c in range(4):
                    for k in range(KC):
                        mm = pe.matmul(bank[:, c:c + 1], w[:, k, c * P:(c + 1) * P], condT[:, k:k + 1],
                                       start=(k == 0), stop=(k == KC - 1))
                full(mm, f"ada{g}")
                last_of(f"ada{g}", f"ada{g}")
            ada.g += n
        ada.g = 0

        for l in range(DEPTH):
            L = f"{l}."
            pe.wait_ge(ev("h_ready"), l + 1)
            for g, name in enumerate(("q", "k")):
                w = weights(f"{name}{l}")
                for j in range(2):
                    features(f"{L}{name}{j}", w, hT, 256 * j, 2)
                last_of(f"{name}{l}", f"{L}{name}1")
            w = weights(f"va{l}")
            for b in range(NB):
                tokens(f"{L}va{b}", w, hT, b, 0, 512)
            last_of(f"va{l}", f"{L}va1")
            for j in range(4):
                read_out(pe, f"{L}{'qk'[j // 2]}{j % 2}")
                bank = take(f"{L}rot{j}")
                mm = pe.matmul(bank[:, :], K["rot"][:, :],
                               qk_raw[:, 2 * j:2 * j + 2, :], start=True, stop=True)
                full(mm, f"{L}rot{j}")
            w = weights(f"ga{l}")
            for j in range(2):
                features(f"{L}ga{j}", w, hT, 256 * j, 2)
            last_of(f"ga{l}", f"{L}ga1")
            w = weights(f"bqk{l}")
            for j in range(2):
                features(f"{L}bqk{j}", w, hT, 256 * j, 2)
            last_of(f"bqk{l}", f"{L}bqk1")
            w = weights(f"bvfg{l}")
            for b in range(NB):
                tokens(f"{L}bv{b}", w, hT, b, 0, 256 + HB)
            features(f"{L}gb", w, hT, 256 + HB, 2)
            last_of(f"bvfg{l}", f"{L}gb")
            w = weights(f"cqk{l}")
            for j in range(2):
                features(f"{L}cqk{j}", w, hT, 256 * j, 2)
            last_of(f"cqk{l}", f"{L}cqk1")
            w = weights(f"cvg{l}")
            for b in range(NB):
                tokens(f"{L}cv{b}", w, hT, b, 0, 256)
            features(f"{L}gc", w, hT, 256, 2)
            last_of(f"cvg{l}", f"{L}gc")

            pe.wait_ge(ev("rope"), 4 * l + 4)
            for h in range(HA):
                for m in range(2):
                    head_rows(f"{L}s{h}{m}", qk, h, qk, 4 + h, m)
            read_out(pe, f"{L}cqk1")
            for h in range(HC):
                name, r = f"{L}z{h}", slice(h % 2 * HEAD, h % 2 * HEAD + HEAD)
                bank = take(name)
                pe.matmul(bank[:, 0:T], bc_qk[r, 6 + h // 2, 0:P], bc_qk[r, 4 + h // 2, :],
                          start=True, stop=True)
                mm = pe.matmul(bank[:, T:W3], bc_qk[r, 6 + h // 2, P:T], bc_qk[r, 4 + h // 2, P:T],
                               start=True, stop=True)
                full(mm, name)
            ada(3)
            pe.wait_ge(ev("logf"), l + 1)
            bank = take(f"{L}cumq")
            pe.matmul(bank[:, 0:HB], up, logf[:, 0, :], start=True, stop=True)
            pe.matmul(bank[:, HB:2 * HB], ones, logf[:, 0, :], start=True, stop=False)
            mm = pe.matmul(bank[:, HB:2 * HB], up, logf[:, 1, :], start=False, stop=True)
            full(mm, f"{L}cumq")
            for h in range(HB):
                if h % 2 == 0:
                    bank = take(f"{L}cumk{h // 2}")
                c = h % 2 * T
                pe.matmul(bank[:, c:c + T], logf[:, 0, h:h + 1].broadcast_to([P, P]), up_ones[:, :],
                          start=True, stop=False)
                mm = pe.matmul(bank[:, c + P:c + T], logf[:, 1, h:h + 1].broadcast_to([P, P]), up,
                               start=False, stop=True)
                if h % 2:
                    full(mm, f"{L}cumk{h // 2}")
            for h in range(HB):
                head_rows(f"{L}f{h}", bc_qk, h // 2, bc_qk, 2 + h // 2, h % 2)
            pe.wait_ge(ev("log_fail"), l + 1)
            for h in range(HC):
                bank = take(f"{L}after{h}")
                pe.matmul(bank[:, 0:W3], K["down"][:, :], ls[:, h, :], start=True, stop=False)
                mm = pe.matmul(bank[:, P:T], ones, ls[:, h, T:W3], start=False, stop=True)
                full(mm, f"{L}after{h}")
            ada(3)
            def turn_a(h):
                pe.wait_ge(ev("wa"), HA * l + h + 1)
                turn_rows(f"{L}at{h}", sc[:, 2 * h, :])

            def turn_f(h):
                pe.wait_ge(ev("wf"), HB * l + h + 1)
                turn_rows(f"{L}ft{h}", sf[:, h, :])

            head_values(f"{L}a", HA, turn_a, va, lambda h: slice(h * P, (h + 1) * P), probT, 0,
                        lambda h: f"{L}oa{h // 2}", lambda h: (h % 2, None))
            head_values(f"{L}f", HB, turn_f, vbc, lambda h: slice(h * HEAD, (h + 1) * HEAD), probT, HA,
                        lambda h: f"{L}ob", lambda h: (h // 2, h % 2))
            o_bank = take(f"{L}oc")
            pe.wait_ge(ev("wc"), l + 1)
            for h in range(HC):
                mm = apply_values(o_bank, h // 2, vbc, slice(256 + h * HEAD, 256 + (h + 1) * HEAD),
                                  zs[:, h, :], h % 2)
            full(mm, f"{L}oc")
            pe.wait_ge(ev("sq_a"), l + 1)
            for j in range(2):
                bank = take(f"{L}ms{j}")
                mm = pe.matmul(bank[:, :], means[:, 1, :], wide[:, 2 * j:2 * j + 2, :], start=True, stop=True)
                full(mm, f"{L}ms{j}")
            pe.wait_ge(ev("y_ready"), l + 1)
            for j in range(2):
                w = weights(f"out{l}.{j}")
                for i in range(2):
                    features(f"{L}out{2 * j + i}", w, yT, 256 * i, 2)
                last_of(f"out{l}.{j}", f"{L}out{2 * j + 1}")
            norm_sums(L, xT, f"{L}out3")

        norm_sums("m.", xT, None)
        pe.wait_ge(ev("h_ready"), DEPTH + 2)
        w = weights("q2")
        for j in range(2):
            features(f"q2.{j}", w, hT, 256 * j, 2)
        last_of("q2", "q2.1")
        w = weights("kvqi")
        features("kvl", w, hT, 0, 2)
        features("qi0", w, hT, 256, 2)
        last_of("kvqi", "qi0")
        w = weights("qkwi")
        features("qi1", w, hT, 0, 2)
        bank = take("ki")
        for half in range(2):
            for k in range(KC):
                mm = pe.matmul(bank[half * HEAD:(half + 1) * HEAD, 0:T], w[:, k, 256:320], hT[:, k, :],
                               start=(k == 0), stop=(k == KC - 1))
        full(mm, "ki")
        bank = take("wi")
        for b in range(NB):
            for k in range(KC):
                mm = pe.matmul(bank[:, b * AH:(b + 1) * AH], hT[:, k, b * P:(b + 1) * P], w[:, k, 320:328],
                               start=(k == 0), stop=(k == KC - 1))
        full(mm, "wi")
        last_of("qkwi", "wi")
        for j in range(3):
            w = weights(f"x{j}")
            for i in range(2):
                features(f"xbc{2 * j + i}", w, hT, 256 * i, 2)
            last_of(f"x{j}", f"xbc{2 * j + 1}")
        w = weights("dtg")
        bank = take("dt")
        for b in range(NB):
            for k in range(KC):
                mm = pe.matmul(bank[:, b * SH:(b + 1) * SH], hT[:, k, b * P:(b + 1) * P], w[:, k, 0:SH],
                               start=(k == 0), stop=(k == KC - 1))
        full(mm, "dt")
        for i in range(2):
            features(f"g{i}", w, hT, SH + 256 * i, 2)
        last_of("dtg", "g1")
        pe.wait_ge(ev("sq_q"), 1)
        for j in range(2):
            bank = take(f"q2ms{j}")
            mm = pe.matmul(bank[:, :], K["half"][:, :], wide[:, 2 * j:2 * j + 2, :], start=True, stop=True)
            full(mm, f"q2ms{j}")
        pe.wait_ge(ev("sq_kv"), 1)
        sum_chunks("kvms", wide, [range(4, 6)], means[:, 2, :])
        read_out(pe, "ki")
        bank = take("kimean")
        mm = pe.matmul(bank[:, 0:T], K["half"][:, :], ki[:, :], start=True, stop=True)
        full(mm, "kimean")
        pe.wait_ge(ev("sq_ki"), 1)
        bank = take("kivar")
        mm = pe.matmul(bank[:, 0:T], K["half"][:, :], wide[:, 6, :], start=True, stop=True)
        full(mm, "kivar")
        for j in range(2):
            w = weights(f"z{j}")
            for i in range(2):
                features(f"z{2 * j + i}", w, hT, 256 * i, 2)
            last_of(f"z{j}", f"z{2 * j + 1}")
        w = weights("kvup")
        pe.wait_ge(ev("kvl"), 2)
        for j in range(2):
            features(f"k2.{j}", w, kvl, 256 * j, 2)
        for b in range(NB):
            tokens(f"v2.{b}", w, kvl, b, 512, 512)
        last_of("kvup", "v2.1")
        pe.wait_ge(ev("ki"), 1)
        for h in range(AH):
            name, r = f"is{h}", slice(h % 2 * HEAD, h % 2 * HEAD + HEAD)
            bank = take(name)
            pe.matmul(bank[:, 0:P], qi[r, h // 2, 0:P], ki[r, 0:P], start=True, stop=True)
            mm = pe.matmul(bank[:, P:W3], qi[r, h // 2, P:T], ki[r, 0:T], start=True, stop=True)
            full(mm, name)
        pe.wait_ge(ev("sq_k"), 1)
        for j in range(2):
            bank = take(f"k2ms{j}")
            mm = pe.matmul(bank[:, :], K["half"][:, :], wide[:, 2 * j:2 * j + 2, :], start=True, stop=True)
            full(mm, f"k2ms{j}")
        pe.wait_ge(ev("dta"), 1)
        bank = take("acum")
        for b in range(NB):
            pe.matmul(bank[:, b * SH:(b + 1) * SH], up, dta[:, b, :], start=True, stop=True)
        mm = pe.matmul(bank[:, 2 * SH:3 * SH], ones, dta[:, 0, :], start=True, stop=True)
        full(mm, "acum")
        pe.wait_ge(ev("xs"), 1)
        for b in range(NB):
            for j in range(2):
                bank = take(f"xt{b}{j}")
                for i in range(4):
                    mm = pe.transpose(bank[:, i * P:(i + 1) * P], xbcs[:, 4 * j + i, b * P:(b + 1) * P], ident[:, :])
                full(mm, f"xt{b}{j}")
        for g in range(2):
            bank = take(f"cb{g}")
            pe.matmul(bank[:, 0:T], xbcs[:, 8 + g, 0:P], xbcs[:, 10 + g, :], start=True, stop=True)
            mm = pe.matmul(bank[:, T:W3], xbcs[:, 8 + g, P:T], xbcs[:, 10 + g, P:T], start=True, stop=True)
            full(mm, f"cb{g}")
        read_out(pe, "xt11")
        for h in range(SH):
            bank = take(f"A{h}")
            for b in range(NB):
                mm = pe.matmul(bank[:, b * P:(b + 1) * P], dta[:, b, h:h + 1].broadcast_to([P, P]), up,
                               start=True, stop=True)
            full(mm, f"A{h}")
            if h >= 1:
                ssm_values(h - 1)
        ssm_values(SH - 1)
        pe.wait_ge(ev("sq_y"), 1)
        sum_chunks("yms", wide, [range(4), range(4, 8)], means[:, 3, :])
        pe.wait_ge(ev("qk2"), 2)
        for h in range(AH):
            head_rows(f"t{h}", q2, h // 2, k2, h // 2, h % 2)
        for j in range(3):
            w = weights(f"g{j + 1}")
            for i in range(2):
                features(f"g{2 * j + 2 + i}", w, hT, 256 * i, 2)
            last_of(f"g{j + 1}", f"g{2 * j + 3}")
        def turn_2(h):
            pe.wait_ge(ev("w2"), h + 1)
            turn_rows(f"2.t{h}", sc2[:, h, :])

        head_values("2.", AH, turn_2, v2, lambda h: slice(h * HEAD, (h + 1) * HEAD), probT2, 0,
                    lambda h: f"o2.{h // 4}", lambda h: (h // 2 % 2, h % 2))
        w = weights("ao")
        read_out(pe, "o2.1")
        for j in range(4):
            features(f"ya{j}", w, q2, 256 * j, 2)
        last_of("ao", "ya3")
        pe.wait_ge(ev("y_ssm"), 1)
        for j in range(2):
            w = weights(f"so{j}")
            for i in range(2):
                features(f"ys{2 * j + i}", w, yS, 256 * i, 2)
            last_of(f"so{j}", f"ys{2 * j + 1}")
        pe.wait_ge(ev("mixed"), 4)
        for j in range(2):
            w = weights(f"wo{j}")
            for i in range(2):
                features(f"wo{2 * j + i}", w, zg, 256 * i, 2)
            last_of(f"wo{j}", f"wo{2 * j + 1}")
        norm_sums("f.", xT, None)

        pe.wait_ge(ev("h_ready"), DEPTH + 3)
        bank = take("router")
        for b in range(NB):
            for k in range(KC):
                mm = pe.matmul(bank[:, b * NE:(b + 1) * NE], hT[:, k, b * P:(b + 1) * P], w_router[:, k, :],
                               start=(k == 0), stop=(k == KC - 1))
        full(mm, "router")
        for b in range(NB):
            for j in range(2):
                bank = take(f"ht{b}{j}")
                for i in range(4):
                    mm = pe.transpose(bank[:, i * P:(i + 1) * P], hT[:, 4 * j + i, b * P:(b + 1) * P], ident[:, :])
                full(mm, f"ht{b}{j}")
        pe.wait_ge(ev("chosen"), 1)
        bank = take("pos")
        pe.matmul(bank[:, 0:NE], K["before"][:, :], rt[:, 0, 0, :], start=True, stop=True)
        pe.matmul(bank[:, NE:2 * NE], ones, rt[:, 0, 0, :], start=True, stop=False)
        mm = pe.matmul(bank[:, NE:2 * NE], K["before"][:, :], rt[:, 0, 1, :], start=False, stop=True)
        full(mm, "pos")
        bank = take("count")
        for b in range(NB):
            mm = pe.matmul(bank[0:NE, 0:1], rt[:, 0, b, :], ones[:, 0:1], start=(b == 0), stop=(b == NB - 1))
        full(mm, "count")
        bank = take("gateT")
        for b in range(NB):
            mm = pe.transpose(bank[0:NE, b * P:(b + 1) * P], rt[:, 1, b, :], ident[:, :])
        full(mm, "gateT")
        pe.wait_ge(ev("passes"), 1)
        bank = take("cum_passes")
        mm = pe.matmul(bank[0:NE, 0:1], up_ones[0:NE, 0:NE], passes[:, 1:2], start=True, stop=True)
        full(mm, "cum_passes")
        pe.wait_ge(ev("passes"), 2)
        bank = take("todo")
        M = MAX_EXTRA
        pe.matmul(bank[0:1, 0:M], up_ones[0:NE, P:P + 1], passes[:, 4:4 + M], start=True, stop=True)
        pe.matmul(bank[0:1, M:2 * M], passes[:, 1:2], passes[:, 4:4 + M], start=True, stop=True)
        mm = pe.matmul(bank[0:1, 2 * M:2 * M + 1], passes[:, 1:2], up_ones[0:NE, P:P + 1], start=True, stop=True)
        full(mm, "todo")

        for b in range(BANKS):
            uses = len([1 for x, _ in banks.values() if x == b])
            pe.wait_ge(bank_free[b], uses)
        pe.wait_ge(ev("b_dn_in"), 16)
        pe.wait_ge(ev("zero"), 1)
        for j in range(4):
            pe.matmul(psum[:, j, :], zero[:, :], hT[:, 0:2, :], start=True, stop=False, skip_group_check=True)
        for c in range(KC):
            mm = pe.matmul(psum[:, c // 2, c % 2 * T:(c % 2 + 1) * T], b_dn[:, c * P:(c + 1) * P], gateT[:, :],
                           start=False, stop=False, skip_group_check=True)

        def expert(n):
            pe.wait_ge(ev("picked"), n + 1)
            for c in range(KC):
                for b in range(NB):
                    mm = pe.matmul(psum[:, 4, c * CAP:(c + 1) * CAP], h_tok[:, b, c * P:(c + 1) * P],
                                   pick[:, b, :], start=(b == 0), stop=(b == NB - 1))
            mm.then_inc(ev("gathered"), 1)
            for b in range(NB):
                mm = pe.transpose(psum[0:CAP, 7, b * P:(b + 1) * P], pick_gate[:, b, :], ident[:, :])
            mm.then_inc(ev("turned"), 1)
            pe.wait_ge(ev("hg"), n + 1)
            for j in range(4):
                slot = expert_slot[j]
                pe.wait_ge(slot_full[slot], 16 * (slot_uses[slot] + 1) + 16 * n)
                w = slot_view(slot, KC, 512)
                for i in range(4):
                    c = 4 * j + i
                    for k in range(KC):
                        mm = pe.matmul(psum[:, 5 + c // 8, c % 8 * CAP:(c % 8 + 1) * CAP],
                                       w[:, k, i * P:(i + 1) * P], hg[:, k, :],
                                       start=(k == 0), stop=(k == KC - 1))
                mm.then_inc(ev("gu_done"), 1)
            pe.wait_ge(ev("act"), n + 1)
            for j in range(2):
                pe.wait_ge(ev(f"down_in{j}"), 16 * n + 16)
                w = w_down[:, j, :].rearrange("p (k n) -> p k n", k=KC)
                if j == 0:
                    pe.wait_ge(ev("putT"), n + 1)
                for k in range(KC):
                    mm = pe.matmul(psum[0:CAP, 7 if j == 0 else 4, :], actT[:, 2, k, :], w[:, k, :],
                                   start=(k == 0), stop=(k == KC - 1))
                mm.then_inc(ev("down_done"), 1)
            for c in range(KC):
                if c % 4 == 0:
                    pe.wait_ge(ev("o_slot"), 2 * n + c // 4 + 1)
                mm = pe.matmul(psum[:, c // 2, c % 2 * T:(c % 2 + 1) * T], o_slot[:, c * P:(c + 1) * P],
                               putT[:, :], start=False, stop=False, skip_group_check=True)
            mm.then_inc(ev("scattered"), 1)

        with pe.Fori(0, NE) as e:
            expert(e)
        pe.wait_ge(ev("todo"), 1)
        extra = pe.value_load(todo[0:1, 2 * M:2 * M + 1], min_val=0, max_val=M)
        with pe.Fori(0, M) as i:
            with pe.If(extra > i):
                expert(i + NE)
            pe.nop()
        pe.wait_ge(ev("final"), KC)
        for b in range(NB):
            for j in range(2):
                for i in range(4):
                    mm = pe.transpose(psum[:, 4 + 2 * b + j, i * P:(i + 1) * P],
                                      xT[:, 4 * j + i, b * P:(b + 1) * P], ident[:, :])
                mm.then_inc(ev("turned_out"), 1)

    @block.sync
    def _(sp):
        sp.dma_start(x_in[:, :, :], a["x"][0].rearrange("(b p) d -> p b d", p=P)).then_inc(ev("x_in"), 16)
        for name in consts:
            sp.dma_start(K[name][:, :], const_dram[name][:, :]).then_inc(ev("const_in"), 16)
        for g, (name, src) in enumerate(groups):
            slot = g % RING
            if g >= RING:
                sp.wait_ge(*slot_last[g - RING])
            sp.dma_start(slot_view(slot, src.shape[1], src.shape[2]), src).then_inc(slot_full[slot], 16)
            if name == "ada0":
                read_out(sp, "bias")
                sp.dma_start(bias_dram[:, :, :], biasrev[:, :].rearrange("h (o j) -> h o j", o=1)
                             .broadcast_to([AH, P, 2 * T])).then_inc(ev("bias_out"), 16)
            if name == "x0":
                sp.wait_ge(ev("bias_out"), 16)
                sp.wait_ge(ev("h_ready"), DEPTH + 1)
                for qb in range(NB):
                    width = (qb + 1) * P
                    src = bass.AP(tensor=bias_dram[:, :, :].tensor, offset=T - 1 - qb * P,
                                  ap=[[2 * T - 1, P], [P * 2 * T, AH], [1, width]])
                    dst = bm[:, :, 0:P] if qb == 0 else bm[:, :, P:W3]
                    sp.dma_start(dst, src).then_inc(ev("bias_in"), 16)

        def gate_up(n, e, peeled=False):
            for j in range(4):
                slot = expert_slot[j]
                if peeled:
                    sp.wait_ge(*slot_last[NG - RING + j])
                else:
                    sp.wait_ge(ev("gu_done"), 4 * n + j - 3)
                sp.dma_start(slot_view(slot, KC, 512), w_gu[bass.ds(e, 1), :, :, 512 * j:512 * j + 512]
                             .rearrange("e p k n -> (e p) k n")).then_inc(slot_full[slot], 16)

        def down(n, e, peeled=False):
            for j in range(2):
                if not peeled:
                    sp.wait_ge(ev("down_done"), 2 * n + j - 1)
                sp.dma_start(w_down[:, j, :].rearrange("p (k n) -> p k n", k=KC),
                             w_dn[bass.ds(e, 1), :, :, 512 * j:512 * j + 512]
                             .rearrange("e p k n -> (e p) k n")).then_inc(ev(f"down_in{j}"), 16)

        gate_up(0, 0, True)
        sp.wait_ge(ev("h_ready"), DEPTH + 3)
        sp.dma_start(b_dn[:, :], a["b_dn_2"][0]).then_inc(ev("b_dn_in"), 16)
        down(0, 0, True)
        with sp.Fori(1, NE) as e:
            gate_up(e, e)
            down(e, e)
        sp.wait_ge(ev("todo"), 1)
        extra = sp.value_load(todo[0:1, 2 * MAX_EXTRA:2 * MAX_EXTRA + 1], min_val=0, max_val=MAX_EXTRA)
        with sp.Fori(0, MAX_EXTRA) as i:
            with sp.If(extra > i):
                e = sp.value_load(todo[0:1, bass.ds(i, 1)], min_val=0, max_val=NE - 1)
                gate_up(i + NE, e)
                down(i + NE, e)
            sp.nop()
        for b in range(NB):
            sp.wait_ge(ev("out_rows"), 2 * b + 2)
            sp.dma_start(out[0, b * P:(b + 1) * P, :], h_tok[:, b, :]).then_inc(ev("out_done"), 16)
        sp.wait_ge(ev("out_done"), 16 * NB)

    @block.scalar
    def _(act):
        ch = Chain(act, "act_done")

        def f(out_, in_, func, s=None, **kw):
            ch.after(act.activation(out_, in_, func, **kw), s)

        def read(name, out_, func=ACT.Copy, cols=slice(0, 512), rows=slice(0, P), last=True, **kw):
            ins = act.activation(out_, shaped(product(act, name)[rows, cols], out_), func, **kw)
            if last:
                ch.free(ins, name)
            else:
                ch.after(ins)

        for tile, at, n, src in row_loads:
            act.dma_start(vec_rows[at:at + n, tile, :], src).then_inc(ev("rows_in"), 16)
        for at, src in twice:
            for half in range(2):
                act.dma_start(vec_rows[at:at + 1, 1, half * HEAD:(half + 1) * HEAD], src).then_inc(ev("rows_in"), 16)
        act.dma_start(bgu_rows[:, 0:N_BGU, :], a["b_gu_2"][0].rearrange("e (c p) -> (e c) p", p=P)
                      .rearrange("(t r) p -> r t p", r=P)).then_inc(ev("bgu_in"), 16)
        alike = [(lam_in[:, i, :], a[n].rearrange("l d -> (l d)")) for i, n in
                 enumerate(("lambda_q1", "lambda_k1", "lambda_q2", "lambda_k2"))]
        alike += [(b_forget[:, :], a["b_forget"].rearrange("l h -> (l h)")), (dt_bias[:, :], a["dt_bias_2"][0]),
                  (a_log[:, :], a["a_log_2"][0]), (b_router[:, :], a["b_router_2"][0])]
        for dst, src in alike:
            act.dma_start(dst, src.partition_broadcast(P)).then_inc(ev("bcast_in"), 16)
        for half in range(2):
            src = a["d_skip_2"][0].rearrange("(c two) -> two c", two=2)[half]
            with nc.allow_non_contiguous_dma(reason="16 numbers"):
                act.dma_start(d_skip[half * HEAD:(half + 1) * HEAD, :], src.partition_broadcast(HEAD))\
                    .then_inc(ev("bcast_in"), 16)
        act.dma_start(rel_bias[:, :], a["rel_bias_2"]).then_inc(ev("bcast_in"), 16)
        act.dma_start(w_router[:, :, :], a["w_router_2"][0].rearrange("(k p) n -> p k n", p=P))\
            .then_inc(ev("bcast_in"), 16)

        norms = [0]

        def rstd(name, out_, eps_col, s=None, cols=slice(0, 512)):
            read(name, out_, ACT.Ln, cols=cols, bias=eps[:, eps_col:eps_col + 1])
            f(out_, out_, ACT.Exp, s, scale=-0.5)

        def norm(tag, centred, scale, shift, dst, e):
            if centred:
                act.wait_ge(ev("centred"), centred)
            f(wide[:, :, :], xT[:, :, :], ACT.Square, ev("sq_d"))
            rstd(tag + "var", stat[:, :], e, ev("rstd"), cols=slice(0, T))
            norms[0] += 1
            act.wait_ge(ev("scaled"), norms[0])
            for c in range(KC):
                ins = act.activation(dst[:, c, :], dst[:, c, :], ACT.Identity, bias=shift(c), scale=scale(c))
            ins.then_inc(ev("h_ready"), 1)
            act.wait_ge(ev("h_ready"), norms[0])

        act.wait_ge(ev("means_set"), 6)
        read_out(act, "bgu")
        f(condT[:, :], vec("c", 0, 8), ACT.Silu, ev("cond"))
        act.wait_ge(ev("lam_sum"), 1)
        f(lam[:, 0:4], lam[:, 0:4], ACT.Exp, ev("lam_exp"))
        norm("in.", 1, lambda c: vec("ln_in_g", c), lambda c: vec("ln_in_b", c), hT, 0)

        for l in range(DEPTH):
            L = f"{l}."
            for j in range(4):
                read(f"{L}{'qk'[j // 2]}{j % 2}", qk_raw[:, 2 * j:2 * j + 2, :])
            for b in range(NB):
                read(f"{L}va{b}", va[:, b, :])
            for j in range(2):
                read(f"{L}ga{j}", gate[:, 2 * j:2 * j + 2, :], ACT.Silu)
            for j in range(2):
                read(f"{L}bqk{j}", bc_qk[:, 2 * j:2 * j + 2, :])
            for b in range(NB):
                read(f"{L}bv{b}", vbc[:, b, 0:256], cols=slice(0, 256), last=False)
                read(f"{L}bv{b}", logf[:, b, :], cols=slice(256, 256 + HB))
            read(f"{L}gb", gate[:, 4:6, :], ACT.Silu)
            for j in range(2):
                read(f"{L}cqk{j}", bc_qk[:, 4 + 2 * j:6 + 2 * j, :])
            for b in range(NB):
                read(f"{L}cv{b}", vbc[:, b, 256:512], cols=slice(0, 256))
            read(f"{L}gc", gate[:, 6:8, :], ACT.Silu)
            act.wait_ge(ev("forget_x"), l + 1)
            f(small[:, 8:16], small[:, 0:8], ACT.Abs)
            f(small[:, 8:16], small[:, 8:16], ACT.Exp, scale=-1.0)
            f(small[:, 8:16], small[:, 8:16], ACT.Ln, ev("forget_ln"), bias=1.0)
            for h in range(HC):
                read(f"{L}z{h}", zs[:, h, :], cols=slice(0, W3), scale=HEAD ** -0.5)
            f(ls[:, :, :], zs[:, :, :], ACT.Abs)
            f(ls[:, :, :], ls[:, :, :], ACT.Exp, scale=-1.0)
            f(ls[:, :, :], ls[:, :, :], ACT.Ln, ev("c_ln"), bias=1.0)
            act.wait_ge(ev("a_max"), l + 1)
            row_exp(act, sc, 0, 8, row_max, row_sum, 0, 8, ev("a_exp"))
            act.wait_ge(ev("f_max"), l + 1)
            row_exp(act, sf, 0, 4, row_max, row_sum, 16, 20, ev("f_exp"))
            act.wait_ge(ev("c_exponent"), l + 1)
            f(zs[:, :, :], zs[:, :, :], ACT.Exp, ev("wc"))
            for i in range(HA + HB):
                tag, h = ("a", i) if i < HA else ("f", i - HA)
                if i >= 2:
                    before = ("a", i - 2) if i - 2 < HA else ("f", i - 2 - HA)
                    act.wait_ge(*values_done[(L + before[0], before[1])])
                read(f"{L}{tag}t{h}", probT[:, i % 2, :], cols=slice(0, W3))
                if i == 3:
                    read(f"{L}oa0", yT[:, 0:2, :])
                if i == 5:
                    read(f"{L}oa1", yT[:, 2:4, :])
                    f(wide[:, 0:4, :], yT[:, 0:4, :], ACT.Square, ev("sq_a"))
            for j in range(2):
                rstd(f"{L}ms{j}", wide[:, 4 + 2 * j:6 + 2 * j, :], 0, ev("rstd_a"))
            norm(L, l + 2, lambda c: vec("ln_g", 8 * l + c), lambda c: vec("ln_b", 8 * l + c),
                 xT if l == DEPTH - 1 else hT, 0)

        act.wait_ge(ev("mod"), 2)
        norm("m.", None, lambda c: mix_scale[:, c:c + 1], lambda c: modT[:, c:c + 1], hT, 1)
        for j in range(2):
            read(f"q2.{j}", q2[:, 2 * j:2 * j + 2, :])
        f(wide[:, 0:4, :], q2[:, :, :], ACT.Square, ev("sq_q"))
        read("kvl", kvl[:, :, :])
        f(wide[:, 4:6, :], kvl[:, :, :], ACT.Square, ev("sq_kv"))
        for j in range(2):
            read(f"qi{j}", qi[:, 2 * j:2 * j + 2, :], scale=HEAD ** -0.5)
        read("ki", ki[:, :], cols=slice(0, T))
        read("wi", wi[:, :, :], cols=slice(0, 2 * AH), scale=AH ** -0.5)
        for i in range(6):
            read(f"xbc{i}", xbc[:, 2 * i:2 * i + 2, 3:T + 3])
        act.wait_ge(ev("dt_x"), 1)
        f(dtx[:, 1, :], dtx[:, 0, :], ACT.Abs)
        f(dtx[:, 1, :], dtx[:, 1, :], ACT.Exp, ev("dt_u"), scale=-1.0)
        f(exp_a[:, :], a_log[:, :], ACT.Exp)
        act.wait_ge(ev("dt_w"), 1)
        f(dtx[:, 3, :], dtx[:, 2, :], ACT.Ln, ev("dt_ln"))
        for i in range(2):
            read(f"g{i}", ga[:, 2 * i:2 * i + 2, :], ACT.Sigmoid)
        for j in range(2):
            rstd(f"q2ms{j}", wide[:, 2 * j:2 * j + 2, :], 1, ev("rstd_q"))
        rstd("kvms", stat[:, :], 1, ev("rstd_kv"), cols=slice(0, T))
        act.wait_ge(ev("ki_centred"), 1)
        f(wide[:, 6, :], ki[:, :], ACT.Square, ev("sq_ki"))
        rstd("kivar", wide[:, 7, :], 1, ev("rstd_ki"), cols=slice(0, T))
        for i in range(4):
            read(f"z{i}", zg[:, 2 * i:2 * i + 2, :], ACT.Silu)
        for j in range(2):
            read(f"k2.{j}", k2[:, 2 * j:2 * j + 2, :])
        act.wait_ge(ev("qk2"), 1)
        f(wide[:, 0:4, :], k2[:, :, :], ACT.Square, ev("sq_k"))
        for b in range(NB):
            read(f"v2.{b}", v2[:, b, :])
        for h in range(AH):
            if h >= 2:
                act.wait_ge(ev("index_sum"), h - 1)
            read(f"is{h}", idx[:, 1 + h % 2, :], ACT.Relu, cols=slice(0, W3))
        for j in range(2):
            rstd(f"k2ms{j}", wide[:, 2 * j:2 * j + 2, :], 1, ev("rstd_k"))
        for c in range(12):
            act.wait_ge(ev("conv"), c + 1)
            ins = act.activation(xbcs[:, c, :], xbcs[:, c, :], ACT.Silu, bias=vec("conv_b", c))
        ins.then_inc(ev("xs"), 1)
        act.wait_ge(ev("xs"), 1)
        for b in range(NB):
            for j in range(2):
                read(f"xt{b}{j}", x_tok[:, b, 512 * j:512 * j + 512])
        for h in range(SH):
            act.wait_ge(ev("decay_exponent"), h + 1)
            f(decay[:, h % 2, :], decay[:, h % 2, :], ACT.Exp, ev("decay_exp"))
        act.wait_ge(ev("y_gated"), 1)
        f(wide[:, :, :], yS[:, :, :], ACT.Square, ev("sq_y"))
        rstd("yms", wide[:, 0:2, :], 1, ev("rstd_y"))
        act.wait_ge(ev("t_max"), 1)
        row_exp(act, sc2, 0, 8, row_max2, row_sum2, 0, 8, ev("t_exp"))
        for i in range(2, 8):
            if i == 4:
                act.wait_ge(ev("y_ssm"), 1)
            dst = ga[:, 2 * i:2 * i + 2, :] if i < 4 else gs[:, 2 * i - 8:2 * i - 6, :]
            read(f"g{i}", dst, ACT.Sigmoid)
        for h in range(AH):
            if h >= 2:
                act.wait_ge(*values_done[("2.", h - 2)])
            read(f"2.t{h}", probT2[:, h % 2, :], cols=slice(0, W3))
            if h == 5:
                read("o2.0", q2[:, 0:2, :])
        read("o2.1", q2[:, 2:4, :])
        read_out(act, "wo3")
        norm("f.", None, lambda c: mix_scale[:, 8 + c:9 + c], lambda c: modT[:, 24 + c:25 + c], hT, 1)

        act.wait_ge(ev("top"), 1)
        for b in range(NB):
            ins = act.activation(rt[:, 5, b, :], rt[:, 2, b, :], ACT.Exp, bias=rsm[:, 20 + b:21 + b])
        ins.then_inc(ev("gate_exp"), 1)
        for b in range(NB):
            for j in range(2):
                read(f"ht{b}{j}", h_tok[:, b, 512 * j:512 * j + 512])

        def expert(n):
            act.wait_ge(ev("gathered"), n + 1)
            act.activation(hg[:, :, :], psum[:, 4, :].rearrange("p (k s) -> p k s", k=KC), ACT.Copy)\
                .then_inc(ev("hg"), 1)
            act.wait_ge(ev("g_in"), n + 1)
            act.activation(actT[:, 0, :, :], guT[:, 0, :, :], ACT.Sigmoid, scale=1.702).then_inc(ev("g_sig"), 1)
            for j in range(2):
                act.wait_ge(ev("down_done"), 2 * n + j + 1)
                act.activation(o_slot[:, 512 * j:512 * j + 512], psum[0:CAP, 7 if j == 0 else 4, :], ACT.Copy)\
                    .then_inc(ev("o_slot"), 1)

        with act.Fori(0, NE) as e:
            expert(e)
        act.wait_ge(ev("todo"), 1)
        extra = act.value_load(todo[0:1, 2 * MAX_EXTRA:2 * MAX_EXTRA + 1], min_val=0, max_val=MAX_EXTRA)
        with act.Fori(0, MAX_EXTRA) as i:
            with act.If(extra > i):
                expert(i + NE)
            act.nop()
        for b in range(NB):
            for j in range(2):
                act.wait_ge(ev("turned_out"), 2 * b + j + 1)
                act.activation(h_tok[:, b, 512 * j:512 * j + 512], psum[:, 4 + 2 * b + j, :], ACT.Copy)\
                    .then_inc(ev("out_rows"), 1)

    @block.vector
    def _(dve):
        ch = Chain(dve, "dve_done")

        def tt(out_, x, y, op, s=None):
            ch.after(dve.tensor_tensor(out_, x, y, op), s)

        def ts(out_, x, s1, s2, op0, op1=None, s=None, **kw):
            ins = dve.tensor_scalar(out_, x, s1, s2, op0, op1, **kw) if op1 is not None else \
                dve.tensor_scalar(out_, x, s1, None, op0, **kw)
            ch.after(ins, s)

        def stt(out_, x, scalar, y, op0, op1, s=None, **kw):
            ch.after(dve.scalar_tensor_tensor(out_, x, scalar, y, op0, op1, **kw), s)

        def over(v, n):
            return v.rearrange("p (o m) -> p o m", o=1).broadcast_to([v.shape[0], n, v.shape[1]])

        two = lambda v: v.rearrange("p (c t) -> p c t", c=2)

        for i, n in enumerate((D, P, 256, 512)):
            ch.after(dve.memset(means[:, i, :], 1.0 / n), ev("means_set"))
        ch.after(dve.memset(eps[:, 0:1], LN_EPS), ev("means_set"))
        ch.after(dve.memset(eps[:, 1:2], RMS_EPS), ev("means_set"))
        bank = product(dve, "vecs")
        ch.after(dve.tensor_copy(vecs[:, 0, 0:vec_tiles[0]], bank[:, 0:vec_tiles[0]]))
        ch.free(dve.tensor_copy(vecs[:, 1, 0:vec_tiles[1]], bank[:, P:P + vec_tiles[1]]), "vecs")
        ch.free(dve.tensor_copy(bgu[:, :], product(dve, "bgu")), "bgu")
        for c in range(0, KC, 2):
            ch.free(dve.tensor_copy(xT[:, c:c + 2, :], two(product(dve, f"x{c}"))), f"x{c}")
        ch.free(dve.tensor_copy(biasrev[:, :], product(dve, "bias")[0:AH, :]), "bias")
        dve.wait_ge(ev("bcast_in"), 16 * N_BCAST)
        for l in range(DEPTH):
            for i in range(2):
                r = slice(l * HEAD, (l + 1) * HEAD)
                last = l == DEPTH - 1 and i == 1
                stt(small[:, :], lam_in[:, 2 * i, r], 1.0, lam_in[:, 2 * i + 1, r], ALU.mult, ALU.mult,
                    ev("lam_sum") if last else None, accum_out=lam[:, 2 * l + i:2 * l + i + 1])
        dve.wait_ge(ev("lam_exp"), 1)
        for l in range(DEPTH):
            start = layer_lambda(l)
            stt(lam[:, 4 + l:5 + l], lam[:, 2 * l + 1:2 * l + 2], -start, lam[:, 2 * l:2 * l + 1],
                ALU.add, ALU.subtract)
            ts(lam[:, 6 + l:7 + l], vec("subln_g", l), 1.0 - start, None, ALU.mult)

        norms = [0]

        def norm(tag, centred, src, dst):
            if centred:
                mean = product(dve, tag + "mean")[:, 0:T]
                ins = dve.tensor_tensor(xT[:, :, :], xT[:, :, :], over(mean, KC), ALU.subtract)
                ch.after(ins, ev("centred"))
                ch.free(dve.tensor_copy(sink[:, :], mean[:, 0:1]), tag + "mean")
            norms[0] += 1
            dve.wait_ge(ev("rstd"), norms[0])
            tt(dst[:, :, :], xT[:, :, :], over(stat[:, :], KC), ALU.mult, ev("scaled"))

        norm("in.", True, xT, hT)
        ada = [0]

        def read_ada(n):
            for g in range(ada[0], ada[0] + n):
                ch.free(dve.tensor_tensor(modT[:, 4 * g:4 * g + 4], product(dve, f"ada{g}")[:, 0:4],
                                          vec("b_ada", 4 * g, 4), ALU.add), f"ada{g}")
            ada[0] += n

        def maxima(src, n, cols, c0, c1, s):
            ch.after(dve.tensor_reduce(cols[:, c0:c0 + n], src[:, 0:n, 0:P], AX_X, ALU.max))
            ch.after(dve.tensor_reduce(cols[:, c1:c1 + n], src[:, 0:n, P:W3], AX_X, ALU.max))
            ts(cols[:, c0:c1 + n], cols[:, c0:c1 + n], -1.0, None, ALU.mult, s=s)

        PARTS = ((slice(0, P), 0), (slice(P, W3), 1))

        for l in range(DEPTH):
            L = f"{l}."
            for j in range(4):
                rot = product(dve, f"{L}rot{j}")
                ch.free(dve.tensor_tensor(wide[:, 0:2, :], two(rot), over(K["sin"][:, :], 2), ALU.mult), f"{L}rot{j}")
                tt(qk[:, 2 * j:2 * j + 2, :], qk_raw[:, 2 * j:2 * j + 2, :], over(K["cos"][:, :], 2), ALU.mult)
                tt(qk[:, 2 * j:2 * j + 2, :], qk[:, 2 * j:2 * j + 2, :], wide[:, 0:2, :], ALU.add, ev("rope"))
            read_out(dve, f"{L}bv1")
            tt(small[:, 0:8].rearrange("p (b h) -> p b h", b=NB), logf[:, :, :],
               over(b_forget[:, l * HB:(l + 1) * HB], NB), ALU.add, ev("forget_x"))
            dve.wait_ge(ev("forget_ln"), l + 1)
            stt(logf[:, :, :].rearrange("p b h -> p (b h)"), small[:, 0:8], 0.0, small[:, 8:16],
                ALU.min, ALU.subtract, ev("logf"))
            for i in range(2 * HA):
                name = f"{L}s{i // 2}{i % 2}"
                ch.free(dve.scalar_tensor_tensor(sc[:, i, :], product(dve, name)[:, 0:W3], HEAD ** -0.5,
                                                 K["row_mask"][:, :], ALU.mult, ALU.add), name)
            maxima(sc, 8, row_max, 0, 8, ev("a_max"))
            dve.wait_ge(ev("c_ln"), l + 1)
            stt(flat(ls), flat(zs), 0.0, flat(ls), ALU.max, ALU.add)
            tt(ls[:, :, :], ls[:, :, :], over(K["strict_neg"][:, :], 4), ALU.mult, ev("log_fail"))
            read_ada(3)
            ch.free(dve.tensor_copy(cumq[:, :], product(dve, f"{L}cumq")[:, 0:NB * HB]), f"{L}cumq")
            for h in range(HB):
                name = f"{L}cumk{h // 2}"
                cum = product(dve, name)[:, h % 2 * T:(h % 2 + 1) * T]
                ts(sf[:, h, 0:P], cum[:, 0:P], -1.0, cumq[:, h:h + 1], ALU.mult, ALU.add)
                ins = dve.tensor_scalar(sf[:, h, P:W3], cum, -1.0, cumq[:, HB + h:HB + h + 1], ALU.mult, ALU.add)
                if h % 2:
                    ch.free(ins, name)
                else:
                    ch.after(ins)
            tt(sf[:, :, :], sf[:, :, :], over(K["row_mask"][:, :], HB), ALU.add)
            for h in range(HB):
                name = f"{L}f{h}"
                ch.free(dve.scalar_tensor_tensor(sf[:, h, :], product(dve, name)[:, 0:W3], HEAD ** -0.5,
                                                 sf[:, h, :], ALU.mult, ALU.add), name)
            maxima(sf, 4, row_max, 16, 20, ev("f_max"))
            for h in range(HC):
                name = f"{L}after{h}"
                ch.free(dve.tensor_tensor(zs[:, h, :], product(dve, name)[:, 0:W3], zs[:, h, :], ALU.add), name)
            tt(zs[:, :, :], zs[:, :, :], over(K["strict_add"][:, :], 4), ALU.add, ev("c_exponent"))
            read_ada(3)
            dve.wait_ge(ev("a_exp"), l + 1)
            ch.after(dve.reciprocal(small[:, 16:32], row_sum[:, 0:16]))
            ts(small[:, 32:48], small[:, 16:32], lam[:, 4 + l:5 + l], None, ALU.mult)
            for h in range(HA):
                for cols, q in PARTS:
                    r1, r2 = 16 + 8 * q + 2 * h, 32 + 8 * q + 2 * h + 1
                    ts(sc[:, 2 * h + 1, cols], sc[:, 2 * h + 1, cols], small[:, r2:r2 + 1], None, ALU.mult)
                    stt(sc[:, 2 * h, cols], sc[:, 2 * h, cols], small[:, r1:r1 + 1], sc[:, 2 * h + 1, cols],
                        ALU.mult, ALU.add, ev("wa") if q else None)
            dve.wait_ge(ev("f_exp"), l + 1)
            ch.after(dve.reciprocal(row_sum[:, 16:24], row_sum[:, 16:24]))
            for h in range(HB):
                for cols, q in PARTS:
                    ts(sf[:, h, cols], sf[:, h, cols], row_sum[:, 16 + 4 * q + h:17 + 4 * q + h], None, ALU.mult,
                       s=ev("wf") if q else None)
            for name, c in (("ob", 4), ("oc", 6)):
                ch.free(dve.tensor_tensor(yT[:, c:c + 2, :], two(product(dve, L + name)), gate[:, c:c + 2, :],
                                          ALU.mult), L + name)
            dve.wait_ge(ev("rstd_a"), 2 * l + 2)
            stt(flat(yT[:, 0:4, :]), flat(yT[:, 0:4, :]), lam[:, 6 + l:7 + l], flat(wide[:, 4:8, :]), ALU.mult, ALU.mult)
            tt(yT[:, 0:4, :], yT[:, 0:4, :], gate[:, 0:4, :], ALU.mult, ev("y_ready"))
            for j in range(4):
                name = f"{L}out{j}"
                ch.free(dve.scalar_tensor_tensor(flat(xT[:, 2 * j:2 * j + 2, :]), flat(hT[:, 2 * j:2 * j + 2, :]),
                                                 alpha, product(dve, name), ALU.mult, ALU.add), name)
            norm(L, True, xT, xT if l == DEPTH - 1 else hT)

        for i, (norm_name, at) in enumerate((("norm_mix", 8), ("norm_ffn", 32))):
            stt(mix_scale[:, 8 * i:8 * i + 8], modT[:, at:at + 8], 1.0, vec(norm_name, 0, 8), ALU.add, ALU.mult,
                ev("mod"))
        norm("m.", False, xT, hT)
        ch.after(dve.memset(xbc[:, :, 0:3], 0.0))
        ch.free(dve.tensor_tensor(dtx[:, 0, :].rearrange("p (b h) -> p b h", b=NB),
                                  product(dve, "dt")[:, 0:2 * SH].rearrange("p (b h) -> p b h", b=NB),
                                  over(dt_bias[:, :], NB), ALU.add), "dt")
        ts(dt2(dt), dtx[:, 0, :], 0.0, None, ALU.max, s=ev("dt_x"))
        dve.wait_ge(ev("dt_u"), 1)
        ts(dtx[:, 2, :], dtx[:, 1, :], 1.0, None, ALU.add, s=ev("dt_w"))
        stt(dtx[:, 0, :], dtx[:, 2, :], -1.0, dtx[:, 1, :], ALU.add, ALU.subtract)
        dve.wait_ge(ev("dt_ln"), 1)
        tt(dt2(dt), dt2(dt), dtx[:, 3, :], ALU.add)
        ch.after(dve.reciprocal(dtx[:, 3, :], dtx[:, 2, :]))
        tt(dtx[:, 0, :], dtx[:, 0, :], dtx[:, 3, :], ALU.mult)
        tt(dt2(dt), dt2(dt), dtx[:, 0, :], ALU.subtract)
        stt_neg = dve.scalar_tensor_tensor(dta[:, :, :], dt[:, :, :], -1.0, over(exp_a[:, :], NB), ALU.mult, ALU.mult)
        ch.after(stt_neg, ev("dta"))
        dve.wait_ge(ev("rstd_q"), 2)
        stt(flat(q2), flat(q2), vec("q_norm_2"), flat(wide[:, 0:4, :]), ALU.mult, ALU.mult, ev("qk2"))
        ch.free(dve.tensor_tensor(ki[:, :], ki[:, :], product(dve, "kimean")[:, 0:T], ALU.subtract), "kimean")
        ch.after(dve.tensor_copy(sink[:, :], ki[:, 0:1]), ev("ki_centred"))
        dve.wait_ge(ev("rstd_kv"), 1)
        for c in range(2):
            stt(kvl[:, c, :], kvl[:, c, :], vec("kv_norm", c), stat[:, :], ALU.mult, ALU.mult, ev("kvl"))
        dve.wait_ge(ev("rstd_ki"), 1)
        tt(ki[:, :], ki[:, :], wide[:, 7, :], ALU.mult)
        ts(ki[:, :], ki[:, :], vec("idx_k_ln_w_2"), vec("idx_k_ln_b_2"), ALU.mult, ALU.add, s=ev("ki"))
        for h in range(AH):
            read_out(dve, f"is{h}")
            for cols, q in PARTS:
                r, w = idx[:, 1 + h % 2, cols], wi[:, q, h:h + 1]
                s = ev("index_sum") if q else None
                if h == 0:
                    ts(idx[:, 0, cols], r, w, None, ALU.mult, s=s)
                else:
                    stt(idx[:, 0, cols], r, w, idx[:, 0, cols], ALU.mult, ALU.add, s)
        dve.wait_ge(ev("rstd_k"), 2)
        stt(flat(k2), flat(k2), vec("k_norm_2"), flat(wide[:, 0:4, :]), ALU.mult, ALU.mult, ev("qk2"))
        read_out(dve, "xbc5")
        for c in range(12):
            ts(xbcs[:, c, :], xbc[:, c, 0:T], vec("conv_w", c), None, ALU.mult)
            for k in range(1, 4):
                stt(xbcs[:, c, :], xbc[:, c, k:k + T], vec("conv_w", 12 * k + c), xbcs[:, c, :], ALU.mult, ALU.add,
                    ev("conv") if k == 3 else None)
        sums = product(dve, "acum")
        ts(neg_acum[:, 0:2, :].rearrange("p b h -> p (b h)"), sums[:, 0:2 * SH], -1.0, None, ALU.mult)
        ch.free(dve.tensor_tensor(neg_acum[:, 2, :], sums[:, 2 * SH:3 * SH], neg_acum[:, 0, :], ALU.add), "acum")

        for g in range(2):
            ch.free(dve.tensor_copy(cbs[:, g, :], product(dve, f"cb{g}")[:, 0:W3]), f"cb{g}")

        def decay_in(h):
            A, d = product(dve, f"A{h}"), decay[:, h % 2, :]
            if h >= 2:
                dve.wait_ge(*values_done[("ssm", h - 2)])
            col = K["col_mask"][:, 0:P]
            stt(d[:, 0:P], A[:, 0:P], neg_acum[:, 0, h:h + 1], col, ALU.add, ALU.add)
            ts(d[:, P:T], A[:, P:T], neg_acum[:, 2, h:h + 1], None, ALU.add)
            ch.free(dve.scalar_tensor_tensor(d[:, T:W3], A[:, P:T], neg_acum[:, 1, h:h + 1], col, ALU.add, ALU.add),
                    f"A{h}")
            ch.after(dve.tensor_copy(sink[:, :], d[:, 0:1]), ev("decay_exponent"))

        def decay_out(h):
            d, cb = decay[:, h % 2, :], cbs[:, h // 8, :]
            dve.wait_ge(ev("decay_exp"), h + 1)
            stt(d[:, 0:T], d[:, 0:T], dt[:, 0, h:h + 1], cb[:, 0:T], ALU.mult, ALU.mult)
            stt(d[:, T:W3], d[:, T:W3], dt[:, 1, h:h + 1], cb[:, T:W3], ALU.mult, ALU.mult, ev("decay"))
            if h % 4 == 3:
                name = f"yssm{h // 4}"
                y = product(dve, name)
                for i in range(2):
                    c = h // 4 * 2 + i
                    ins = dve.scalar_tensor_tensor(yS[:, c, :], xbcs[:, c, :], d_skip[:, c:c + 1],
                                                   y[:, i * T:(i + 1) * T], ALU.mult, ALU.add)
                    if i:
                        ch.free(ins, name)
                    else:
                        ch.after(ins)

        for h in range(SH + 1):
            if h < SH:
                decay_in(h)
            if h >= 1:
                decay_out(h - 1)
        tt(yS[:, :, :], yS[:, :, :], zg[:, :, :], ALU.mult, ev("y_gated"))

        def top_sum(scores, work, gt, eq, kth, count, need, k):
            ts(gt, scores, kth, 0.0, ALU.is_gt, ALU.add, accum_out=count)
            ts(eq, scores, kth, None, ALU.is_equal)
            ch.after(dve.tensor_tensor_scan(work, eq, eq, 0.0, ALU.add, ALU.max))
            ts(need, count, -1.0, float(k), ALU.mult, ALU.add)
            stt(work, work, need, eq, ALU.is_le, ALU.mult)
            tt(work, work, gt, ALU.add)

        tt(idx[:, 0, :], idx[:, 0, :], K["row_mask"][:, :], ALU.add)
        ch.after(dve.tensor_copy(idx[:, 1, :], idx[:, 0, :]))
        for cols, q in PARTS:
            work, best = idx[:, 1, cols], top8[:, q, :]
            for r in range(TOPK // 8):
                ch.after(dve.max(best, work))
                if r < TOPK // 8 - 1:
                    ch.after(dve.match_replace(work, best, work, -3e38))
            top_sum(idx[:, 0, cols], work, idx[:, 2, cols], idx[:, 3, cols], best[:, 7:8],
                    sm[:, q:q + 1], sm[:, 2 + q:3 + q], TOPK)
        ts(idx[:, 1, :], idx[:, 1, :], -1.0, BIG, ALU.add, ALU.mult)
        tt(idx[:, 0, :], idx[:, 1, :], K["row_mask"][:, :], ALU.add)
        dve.wait_ge(ev("bias_in"), 32)
        tt(bm[:, :, :], bm[:, :, :], over(idx[:, 0, :], AH), ALU.add)

        dve.wait_ge(ev("rstd_y"), 1)
        for c in range(KC):
            stt(yS[:, c, :], yS[:, c, :], vec("ssm_norm", c), wide[:, c // 4, :], ALU.mult, ALU.mult,
                ev("y_ssm") if c == KC - 1 else None)
        for h in range(AH):
            name = f"t{h}"
            ch.free(dve.scalar_tensor_tensor(sc2[:, h, :], product(dve, name)[:, 0:W3], HEAD ** -0.5, bm[:, h, :],
                                             ALU.mult, ALU.add), name)
        maxima(sc2, 8, row_max2, 0, 8, ev("t_max"))
        dve.wait_ge(ev("t_exp"), 1)
        ch.after(dve.reciprocal(row_sum2[:, :], row_sum2[:, :]))
        for h in range(AH):
            for cols, q in PARTS:
                ts(sc2[:, h, cols], sc2[:, h, cols], row_sum2[:, 8 * q + h:8 * q + h + 1], None, ALU.mult,
                   s=ev("w2") if q else None)
        for j in range(4):
            r = slice(2 * j, 2 * j + 2)
            if j == 0:
                read_out(dve, "g3")
            ch.free(dve.tensor_tensor(ga[:, r, :], two(product(dve, f"ya{j}")), ga[:, r, :], ALU.mult), f"ya{j}")
        read_out(dve, "g7")
        for j in range(4):
            r = slice(2 * j, 2 * j + 2)
            ch.free(dve.tensor_tensor(gs[:, r, :], two(product(dve, f"ys{j}")), gs[:, r, :], ALU.mult), f"ys{j}")
            tt(zg[:, r, :], ga[:, r, :], gs[:, r, :], ALU.add, ev("mixed"))
        for j in range(4):
            name = f"wo{j}"
            bank = product(dve, name)
            for i in range(2):
                c = 2 * j + i
                ins = dve.scalar_tensor_tensor(xT[:, c, :], bank[:, i * T:(i + 1) * T], modT[:, 16 + c:17 + c],
                                               xT[:, c, :], ALU.mult, ALU.add)
                if i:
                    ch.free(ins, name)
                else:
                    ch.after(ins)
        norm("f.", False, xT, hT)

        both = lambda v: v.rearrange("p (b e) -> p b e", b=NB)
        ch.after(dve.memset(zero[:, :], 0.0), ev("zero"))
        ch.free(dve.tensor_tensor(rt[:, 2, :, :], both(product(dve, "router")[:, 0:NB * NE]), over(b_router[:, :], NB),
                                  ALU.add), "router")
        for b in range(NB):
            best = rsm[:, 8 * b:8 * b + 8]
            ch.after(dve.max(best, rt[:, 2, b, :]))
            ts(rsm[:, 20 + b:21 + b], best[:, 0:1], -1.0, None, ALU.mult, s=ev("top") if b else None)
        for b in range(NB):
            top_sum(rt[:, 2, b, :], rt[:, 0, b, :], rt[:, 3, b, :], rt[:, 4, b, :],
                    rsm[:, 8 * b + TOPE - 1:8 * b + TOPE], rsm[:, 16 + b:17 + b], rsm[:, 18 + b:19 + b], TOPE)
        dve.wait_ge(ev("gate_exp"), 1)
        for b in range(NB):
            stt(rt[:, 5, b, :], rt[:, 5, b, :], 1.0, rt[:, 0, b, :], ALU.mult, ALU.mult,
                accum_out=rsm[:, 22 + b:23 + b])
        ch.after(dve.reciprocal(rsm[:, 24:26], rsm[:, 22:24]))
        for b in range(NB):
            ts(rt[:, 1, b, :], rt[:, 5, b, :], rsm[:, 24 + b:25 + b], None, ALU.mult, s=ev("chosen") if b else None)
        ch.free(dve.scalar_tensor_tensor(rt[:, 3, :, :], both(product(dve, "pos")[:, 0:NB * NE]), 1.0, rt[:, 0, :, :],
                                         ALU.add, ALU.mult), "pos")
        for r in range(4):
            ts(pos[:, :, r, :], rt[:, 3, :, :], -1.0 - CAP * r, None, ALU.add)
        ch.free(dve.tensor_copy(passes[:, 0:1], product(dve, "count")[0:NE, 0:1]), "count")
        ts(passes[:, 1:2], passes[:, 0:1], CAP + 0.5, None, ALU.is_gt)
        stt(passes[:, 1:2], passes[:, 0:1], 2 * CAP + 0.5, passes[:, 1:2], ALU.is_gt, ALU.add)
        stt(passes[:, 1:2], passes[:, 0:1], 3 * CAP + 0.5, passes[:, 1:2], ALU.is_gt, ALU.add, ev("passes"))
        ch.free(dve.tensor_copy(gateT[:, :], product(dve, "gateT")[0:NE, 0:T]), "gateT")
        ch.free(dve.tensor_copy(passes[:, 2:3], product(dve, "cum_passes")[0:NE, 0:1]), "cum_passes")
        M = MAX_EXTRA
        ts(passes[:, 4:4 + M], K["iota"][0:NE, 0:M], passes[:, 2:3], None, ALU.is_ge, s=ev("passes"))
        bank = product(dve, "todo")
        ch.free(dve.tensor_copy(todo_f[:, 0:2 * M + 1], bank[0:1, 0:2 * M + 1]), "todo")
        stt(todo_f[:, M:2 * M], K["iota"][0:1, 1:M + 1], float(1), todo_f[:, M:2 * M], ALU.mult, ALU.subtract)
        stt(todo_f[:, M:2 * M], todo_f[:, M:2 * M], float(NE), todo_f[:, 0:M], ALU.mult, ALU.add)
        ch.after(dve.tensor_copy(todo[:, 0:2 * M + 1], todo_f[:, 0:2 * M + 1]), ev("todo"))

        pos_at = pos[:, :, :, :].rearrange("p b r e -> p b (r e)")

        def expert(n, e, col):
            for b in range(NB):
                where = pos_at[:, b, bass.ds(col, 1)]
                dve.tensor_scalar(pick[:, b, :], K["iota"][:, :], where, None, ALU.is_equal)
                ins = dve.tensor_scalar(pick_gate[:, b, :], K["iota"][:, :], where, rt[:, 1, b, bass.ds(e, 1)],
                                        ALU.is_equal, ALU.mult)
                if b:
                    ins.then_inc(ev("picked"), 1)
            dve.wait_ge(ev("turned"), n + 1)
            dve.tensor_copy(putT[:, :], psum[0:CAP, 7, 0:T]).then_inc(ev("putT"), 1)
            bias = bgu[:, bass.ds(e * 16, 16)].rearrange("p (c o) -> p c o", o=1)
            for i in range(2):
                gu = guT[:, i, :, :]
                dve.wait_ge(ev("gu_done"), 4 * n + 2 * i + 2)
                dve.tensor_tensor(gu, psum[:, 5 + i, :].rearrange("p (c s) -> p c s", c=KC),
                                  bias[:, 8 * i:8 * i + 8, :].broadcast_to([P, KC, CAP]), ALU.add)\
                    .then_inc(ev("gu_in"), 1)
                dve.wait_ge(ev("gu_in"), 2 * n + i + 1)
                if i == 0:
                    dve.tensor_scalar(gu, gu, 7.0, None, ALU.min).then_inc(ev("g_in"), 1)
                else:
                    dve.tensor_scalar(gu, gu, 7.0, -7.0, ALU.min, ALU.max).then_inc(ev("u_in"), 1)
            dve.wait_ge(ev("u_in"), n + 1)
            dve.scalar_tensor_tensor(flat(actT[:, 1, :, :]), flat(guT[:, 1, :, :]), 1.0, flat(guT[:, 0, :, :]),
                                     ALU.add, ALU.mult).then_inc(ev("ug"), 1)
            dve.wait_ge(ev("ug"), n + 1)
            dve.wait_ge(ev("g_sig"), n + 1)
            dve.tensor_tensor(actT[:, 2, :, :], actT[:, 1, :, :], actT[:, 0, :, :], ALU.mult).then_inc(ev("act"), 1)

        with dve.Fori(0, NE) as e:
            expert(e, e, e)
        extra = dve.value_load(todo[0:1, 2 * M:2 * M + 1], min_val=0, max_val=M)
        with dve.Fori(0, M) as i:
            with dve.If(extra > i):
                e = dve.value_load(todo[0:1, bass.ds(i, 1)], min_val=0, max_val=NE - 1)
                col = dve.value_load(todo[0:1, bass.ds(i + M, 1)], min_val=0, max_val=4 * NE - 1)
                expert(i + NE, e, col)
            dve.nop()
        dve.wait_ge(ev("scattered"), extra + NE)
        for c in range(KC):
            stt(xT[:, c, :], psum[:, c // 2, c % 2 * T:(c % 2 + 1) * T], modT[:, 40 + c:41 + c], xT[:, c, :],
                ALU.mult, ALU.add, ev("final"))

    ctx.close()


_INS = ["x", "ln_in_g", "ln_in_b", "w_in", "b_forget", "lambda_q1", "lambda_k1", "lambda_q2", "lambda_k2", "subln_g",
        "w_out", "ln_g", "ln_b", "c_2", "rel_bias_2", "w_ada_2", "b_ada_2", "norm_mix_2", "norm_ffn_2", "w_in_2",
        "kv_norm_2", "w_kv_up_2", "q_norm_2", "k_norm_2", "idx_k_ln_w_2", "idx_k_ln_b_2", "w_attn_o_2", "conv_w_2",
        "conv_b_2", "dt_bias_2", "a_log_2", "d_skip_2", "ssm_norm_2", "w_ssm_o_2", "w_out_2", "w_router_2",
        "b_router_2", "w_gu_2", "b_gu_2", "w_dn_2", "b_dn_2"]


def kernel(**inputs):
    import numpy as _np
    import concourse.bacc as _bacc
    from concourse import mybir as _mybir
    from concourse.bass_utils import run_bass_kernel_spmd as _run

    nc = _bacc.Bacc("TRN2", target_bir_lowering=False, num_devices=1)
    arrays, aps = {}, {}
    for name in _INS:
        arr = _np.ascontiguousarray(inputs[name])
        arrays[f"in_{name}"] = arr
        aps[name] = nc.dram_tensor(f"in_{name}", arr.shape, _mybir.dt.from_np(arr.dtype), kind="ExternalInput").ap()
    out = nc.dram_tensor("out", inputs["x"].shape, _mybir.dt.float32, kind="ExternalOutput").ap()
    mixer_moe_kernel(nc, aps, out)
    r = _run(nc, [arrays], core_ids=[0])
    return r.results[0]["out"]
```

```python
import math
from contextlib import ExitStack

import numpy as np

import concourse.bass as bass
from concourse import mybir

F32 = mybir.dt.float32
I32 = mybir.dt.int32
ALU = mybir.AluOpType
ACT = mybir.ActivationFunctionType
AX_X = mybir.AxisListType.X

P = 128
BIG = 1e30
RING = 4
BANKS = 7
CAP = 64
LN_EPS = 1e-5
RMS_EPS = 1e-6
HEAD = 64


def layer_lambda(layer):
    return 0.8 - 0.6 * math.exp(-0.3 * layer)


def constants(T):
    i = np.arange(P)
    f = np.float32
    up = (i[:, None] <= i[None, :]).astype(f)
    ones = np.ones((P, P), f)
    half = (i[:, None] // HEAD == i[None, :] // HEAD).astype(f)
    rot = np.zeros((P, P), f)
    for h in range(2):
        for j in range(8):
            rot[h * HEAD + 8 + j, h * HEAD + j] = -1.0
            rot[h * HEAD + j, h * HEAD + 8 + j] = 1.0
    inv = f(500000.0) ** (-np.arange(0, 16, 2, dtype=f) / f(16))
    ang = np.arange(T, dtype=f)[:, None] * inv[None, :].astype(f)
    cos = np.ones((P, T), f)
    sin = np.zeros((P, T), f)
    for h in range(2):
        for part in range(2):
            a = h * HEAD + 8 * part
            cos[a:a + 8] = np.cos(ang).T
            sin[a:a + 8] = np.sin(ang).T
    tri = np.where(i[None, :] <= i[:, None], 0.0, -BIG).astype(f)
    row_mask = np.concatenate([tri, np.zeros((P, P), f), tri], 1)
    col = np.where(i[:, None] <= i[None, :], 0.0, -BIG).astype(f)
    col_mask = np.concatenate([col, np.zeros((P, P), f), col], 1)
    strict = (i[:, None] < i[None, :]).astype(f)
    strict_neg = -np.concatenate([strict, ones, strict], 1)
    strict_add = np.where(strict_neg < 0, 0.0, -BIG).astype(f)
    dist = np.maximum(T - 1 - np.arange(2 * T), 0)
    n = np.maximum(dist, 1).astype(f)
    large = 16 + (np.log(n / 16) / math.log(8.0) * 16).astype(np.int32)
    bucket = np.where(dist < 16, dist, np.minimum(large, 31))
    hot = np.zeros((P, 2 * T), f)
    hot[bucket, np.arange(2 * T)] = 1.0
    mod_sum = np.zeros((P, 12), f)
    for g in range(12):
        mod_sum[g::32, g] = 1.0
    iota = np.tile(np.arange(CAP, dtype=f), (P, 1))
    return {
        "ident": np.eye(P, dtype=f), "up_ones": np.concatenate([up, ones], 1), "down": up.T.copy(),
        "half": half / HEAD, "rot": rot, "cos": cos, "sin": sin,
        "row_mask": row_mask, "col_mask": col_mask, "strict_neg": strict_neg,
        "strict_add": strict_add, "hot": hot, "iota": iota,
        "mod_sum": mod_sum, "before": up - np.eye(P, dtype=f),
    }


def mixer_moe_kernel(nc, a, out):
    T, D = a["x"].shape[1:]
    NB = T // P
    KC = D // P
    DEPTH = a["w_in"].shape[0]
    NE = a["w_gu_2"].shape[1]
    DE = a["w_dn_2"].shape[2]
    assert (T, D, NB, KC, DE) == (256, 1024, 2, 8, 1024)
    HA, HB, HC = 4, 4, 4
    AH, SH = 8, 16
    TOPK, TOPE = 64, 4
    alpha = (2 * DEPTH) ** 0.25
    W3 = 3 * P
    COLS = 528
    MAX_EXTRA = (TOPE * T - 1) // (CAP + 1)

    ctx = ExitStack()

    def sem(name):
        return ctx.enter_context(nc.semaphore(name))

    def sb(name, shape, dt=F32, where=ctx):
        return where.enter_context(nc.sbuf_tensor(name, shape, dt))

    consts = constants(T)
    FIRST_CONSTS = ("hot", "rot", "cos", "sin", "strict_neg", "strict_add")
    K, packs = {}, {}
    for pack in (False, True):
        names = [n for n in consts if (n in FIRST_CONSTS) == pack]
        packs[pack] = (names, nc.inline_tensor(np.concatenate([consts[n] for n in names], 1),
                                               name="c_first" if pack else "c_all"))

    def place_pack(pack, where):
        names, dram = packs[pack]
        tile = sb("k_first" if pack else "k_all", list(dram.shape), where=where)
        at = 0
        for n in names:
            w = consts[n].shape[1]
            K[n] = tile[:, at:at + w]
            at += w
        return tile

    const_tiles = {False: place_pack(False, ctx)}
    ident, up_ones = K["ident"], K["up_ones"]
    up = up_ones[:, 0:P]
    ones = up_ones[:, P:2 * P]

    rows_of = {}
    row_loads = []
    vec_tiles = [0, 0]

    def add_rows(tile, name, source, n):
        rows_of[name] = (tile, vec_tiles[tile])
        row_loads.append((tile, vec_tiles[tile], n, source))
        vec_tiles[tile] += n

    chunk = lambda v: v.rearrange("(c p) -> c p", p=P)
    add_rows(0, "ln_in_g", chunk(a["ln_in_g"]), 8)
    add_rows(0, "ln_in_b", chunk(a["ln_in_b"]), 8)
    add_rows(0, "ln_g", a["ln_g"].rearrange("l (c p) -> (l c) p", p=P), 8 * DEPTH)
    add_rows(0, "ln_b", a["ln_b"].rearrange("l (c p) -> (l c) p", p=P), 8 * DEPTH)
    add_rows(0, "subln_g", a["subln_g"], DEPTH)
    add_rows(0, "norm_mix", chunk(a["norm_mix_2"][0]), 8)
    add_rows(0, "norm_ffn", chunk(a["norm_ffn_2"][0]), 8)
    add_rows(0, "kv_norm", chunk(a["kv_norm_2"][0]), 2)
    add_rows(0, "conv_w", a["conv_w_2"][0].rearrange("k (c p) -> (k c) p", p=P), 48)
    add_rows(1, "conv_b", chunk(a["conv_b_2"][0]), 12)
    add_rows(1, "ssm_norm", chunk(a["ssm_norm_2"][0]), 8)
    add_rows(1, "c", a["c_2"].rearrange("o (c p) -> (o c) p", p=P), 8)
    add_rows(1, "b_ada", a["b_ada_2"].rearrange("o (c p) -> (o c) p", p=P), 48)
    twice = []
    for name in ("q_norm_2", "k_norm_2", "idx_k_ln_w_2", "idx_k_ln_b_2"):
        rows_of[name] = (1, vec_tiles[1])
        twice.append((vec_tiles[1], a[name]))
        vec_tiles[1] += 1
    vecs = sb("vecs", [P, 2, P])

    def vec(name, c=0, n=1):
        tile, at = rows_of[name]
        return vecs[:, tile, at + c:at + c + n]

    b_forget = sb("b_forget", [P, DEPTH * HB])
    dt_bias = sb("dt_bias", [P, SH])
    a_log = sb("a_log", [P, SH])
    b_router = sb("b_router", [P, NE])
    d_skip = sb("d_skip", [P, KC])
    rel_bias = sb("rel_bias", [32, AH])
    biasrev = sb("biasrev", [AH, 2 * T])
    means = sb("means", [P, 4, P])
    eps = sb("eps", [P, 2])
    sink = sb("sink", [P, 1])
    w_router = sb("w_router", [P, KC, NE])

    hT = sb("hT", [P, KC, T])
    xT = sb("xT", [P, KC, T])
    wide = sb("wide", [P, KC, T])
    stat = sb("stat", [P, T])
    modT = sb("modT", [P, 48])
    mix_scale = sb("mix_scale", [P, 16])
    condT = sb("condT", [P, KC, 64])
    mod_rows = sb("mod_rows", [P, 512])
    ring = sb("ring", [P, RING, KC * COLS])

    psum = ctx.enter_context(nc.psum_tensor("psum", [P, BANKS + 1, 512], F32))

    first = ExitStack()
    x_in = sb("x_in", [P, NB, D], where=first)
    const_tiles[True] = place_pack(True, first)
    vec_rows = sb("vec_rows", [P, 2, P], where=first)
    lam_in = sb("lam_in", [P, 4, DEPTH * HEAD], where=first)
    qk_raw = sb("qk_raw", [P, 8, T], where=first)
    qk = sb("qk", [P, 8, T], where=first)
    bc_qk = sb("bc_qk", [P, 8, T], where=first)
    va = sb("va", [P, NB, 512], where=first)
    vbc = sb("vbc", [P, NB, 512], where=first)
    gate = x_in[:, :, :].rearrange("p b d -> p (b d)").rearrange("p (c t) -> p c t", c=KC)
    yT = sb("yT", [P, KC, T], where=first)
    sc = sb("sc", [P, 8, W3], where=first)
    sf = sb("sf", [P, 4, W3], where=first)
    zs = sb("zs", [P, 4, W3], where=first)
    ls = sb("ls", [P, 4, W3], where=first)
    probT = sb("probT", [P, 2, W3], where=first)
    row_max = sb("row_max", [P, 24], where=first)
    row_sum = sb("row_sum", [P, 24], where=first)
    small = sb("small", [P, 64], where=first)
    lam = sb("lam", [P, 8], where=first)
    logf = sb("logf", [P, NB, HB], where=first)
    cumq = sb("cumq", [P, NB * HB], where=first)
    first.close()

    second = ExitStack()
    q2 = sb("q2", [P, 4, T], where=second)
    kvl = sb("kvl", [P, 2, T], where=second)
    qi = sb("qi", [P, 4, T], where=second)
    ki = sb("ki", [P, T], where=second)
    wi = sb("wi", [P, NB, AH], where=second)
    k2 = sb("k2", [P, 4, T], where=second)
    v2 = sb("v2", [P, NB, 512], where=second)
    zg = sb("zg", [P, KC, T], where=second)
    xbc = sb("xbc", [P, 12, T + 3], where=second)
    yS = xbc[:, :, :].rearrange("p c t -> p (c t)")[:, 0:KC * T].rearrange("p (c t) -> p c t", c=KC)
    xbcs = sb("xbcs", [P, 12, T], where=second)
    gs = xbcs[:, 0:KC, :]
    ga = sb("ga", [P, KC, T], where=second)
    sc2 = sb("sc2", [P, 8, W3], where=second)
    early = sc2[:, :, :].rearrange("p h n -> p (h n)")
    x_tok = early[:, 0:NB * D].rearrange("p (b d) -> p b d", b=NB)
    decay = early[:, NB * D:NB * D + 2 * W3].rearrange("p (i n) -> p i n", i=2)
    bm = sb("bm", [P, 8, W3], where=second)
    probT2 = sb("probT2", [P, 2, W3], where=second)
    cbs = sb("cbs", [P, 2, W3], where=second)
    idx = sb("idx", [P, 4, W3], where=second)
    top8 = sb("top8", [P, 2, 8], where=second)
    sm = sb("sm", [P, 16], where=second)
    row_max2 = sb("row_max2", [P, 16], where=second)
    row_sum2 = sb("row_sum2", [P, 16], where=second)
    dtx = sb("dtx", [P, 4, NB * SH], where=second)
    dt = sb("dt", [P, NB, SH], where=second)
    dta = sb("dta", [P, NB, SH], where=second)
    neg_acum = sb("neg_acum", [P, 3, SH], where=second)
    exp_a = sb("exp_a", [P, SH], where=second)
    second.close()

    third = ExitStack()
    h_tok = sb("h_tok", [P, NB, D], where=third)
    w_down = sb("w_down", [P, 2, KC * 512], where=third)
    b_dn = sb("b_dn", [NE, D], where=third)
    hg = sb("hg", [P, KC, CAP], where=third)
    gu = sb("gu", [P, 2, 512], where=third)
    gu_bias = sb("gu_bias", [P, 2, 512], where=third)
    hidden = sb("hidden", [P, 3, 512], where=third)
    o_slot = sb("o_slot", [P, 512], where=third)
    hiddenT = sb("hiddenT", [P, 4, P], where=third)
    pick = sb("pick", [P, NB, CAP], where=third)
    pick_gate = sb("pick_gate", [P, NB, 2, CAP], where=third)
    putT = sb("putT", [P, T], where=third)
    rt = sb("rt", [P, 8, NB, NE], where=third)
    rsm = sb("rsm", [P, 32], where=third)
    pos = sb("pos", [P, NB, 4, NE], where=third)
    gateT = sb("gateT", [NE, T], where=third)
    passes = sb("passes", [NE, 24], where=third)
    todo_f = sb("todo_f", [1, 2 * MAX_EXTRA + 2], where=third)
    todo = sb("todo", [1, 2 * MAX_EXTRA + 2], I32, where=third)
    zero = sb("zero", [P, P], where=third)
    third.close()

    bias_dram = nc.dram_tensor("bias_scratch", (AH, P, 2 * T), F32)

    slot_full = [sem(f"slot_full{i}") for i in range(RING)]
    bank_full = [sem(f"bank_full{i}") for i in range(BANKS)]
    bank_free = [sem(f"bank_free{i}") for i in range(BANKS)]
    events = {}

    def ev(name):
        if name not in events:
            events[name] = sem("e_" + name)
        return events[name]

    groups = []

    def group(name, w, a0, a1):
        groups.append((name, w.rearrange("(k p) n -> p k n", p=P)[:, :, a0:a1]))

    FIRST_GROUPS = [("q", 0, 512), ("k", 512, 1024), ("va", 1024, 1536), ("ga", 1536, 2048),
                    ("bqk", 2048, 2560), ("bvfg", 2560, 3076), ("cqk", 3076, 3588), ("cvg", 3588, 4100)]
    ADA_AT = {"scores": 3, "last": 3}
    ada_next = [0]

    def ada_groups(n):
        for _ in range(n):
            g = ada_next[0]
            group(f"ada{g}", a["w_ada_2"][0], 512 * g, 512 * g + 512)
            ada_next[0] += 1

    for l in range(DEPTH):
        for name, a0, a1 in FIRST_GROUPS:
            group(f"{name}{l}", a["w_in"][l], a0, a1)
        ada_groups(12 // DEPTH)
        for j in range(2):
            group(f"out{l}.{j}", a["w_out"][l], 512 * j, 512 * j + 512)
    for name, a0, a1 in [("q2", 0, 512), ("kvqi", 512, 1024), ("qkwi", 1024, 1352),
                         ("x0", 2376, 2888), ("x1", 2888, 3400), ("x2", 3400, 3912), ("dtg", 3912, 4440),
                         ("z0", 1352, 1864), ("z1", 1864, 2376),
                         ("g1", 4440, 4952), ("g2", 4952, 5464), ("g3", 5464, 5976)]:
        if name == "z0":
            group("kvup", a["w_kv_up_2"][0], 0, 1024)
        group(name, a["w_in_2"][0], a0, a1)
    group("ao", a["w_attn_o_2"][0], 0, 1024)
    for j in range(2):
        group(f"so{j}", a["w_ssm_o_2"][0], 512 * j, 512 * j + 512)
    for j in range(2):
        group(f"wo{j}", a["w_out_2"][0], 512 * j, 512 * j + 512)
    place = {name: g for g, (name, _) in enumerate(groups)}
    NG = len(groups)

    def slot_view(slot, k, n):
        return ring[:, slot, 0:k * n].rearrange("p (k n) -> p k n", k=k)

    expert_slot = [(NG + j) % RING for j in range(4)]
    slot_uses = [len(range(s, NG, RING)) for s in range(RING)]
    w_gu = a["w_gu_2"][0].rearrange("e (k p) n -> e p k n", p=P)
    w_dn = a["w_dn_2"][0].rearrange("e (k p) n -> e p k n", p=P)

    banks = {}
    slot_last = {}

    def product(eng, name):
        b, n = banks[name]
        eng.wait_ge(bank_full[b], n + 1)
        return psum[:, b, :]

    def read_out(eng, name):
        b, n = banks[name]
        eng.wait_ge(bank_free[b], n + 1)

    values_done = {}

    def flat(v):
        v = v[:, :, :] if len(v.shape) == 3 else v
        return v.rearrange("p a b -> p (a b)")

    def dt2(v):
        return v[:, :, :].rearrange("p b h -> p (b h)")

    def shaped(v, like):
        if len(like.shape) == 3:
            return v.rearrange("p (c t) -> p c t", c=like.shape[1])
        return v

    def row_exp(act, scores, h0, n, maxima, sums, c0, c1, s):
        for h in range(n):
            act.activation(scores[:, h, 0:P], scores[:, h, 0:P], ACT.Exp, bias=maxima[:, c0 + h:c0 + h + 1],
                           accum_out=sums[:, c0 + h:c0 + h + 1])
            ins = act.activation(scores[:, h, P:W3], scores[:, h, P:W3], ACT.Exp,
                                 bias=maxima[:, c1 + h:c1 + h + 1], accum_out=sums[:, c1 + h:c1 + h + 1])
        ins.then_inc(s, 1)

    N_BCAST = 12

    class Chain:

        def __init__(self, eng, name):
            self.eng, self.sem, self.count = eng, sem(name), {}

        def after(self, ins, s=None):
            s = self.sem if s is None else s
            ins.then_inc(s, 1)
            key = str(s)
            self.count[key] = self.count.get(key, 0) + 1
            self.eng.wait_ge(s, self.count[key])

        def free(self, ins, name):
            b, n = banks[name]
            ins.then_inc(bank_free[b], 1)
            self.eng.wait_ge(bank_free[b], n + 1)

    block = ctx.enter_context(nc.Block())

    @block.tensor
    def _(pe):
        def take(name):
            n = len(banks)
            banks[name] = (n % BANKS, n // BANKS)
            if n >= BANKS:
                pe.wait_ge(bank_free[n % BANKS], n // BANKS)
            return psum[:, n % BANKS, :]

        def full(mm, name):
            b, n = banks[name]
            mm.then_inc(bank_full[b], 1)

        def weights(name):
            g = place[name]
            pe.wait_ge(slot_full[g % RING], 16 * (g // RING + 1))
            _, src = groups[g]
            return slot_view(g % RING, src.shape[1], src.shape[2])

        def last_of(group_name, product):
            b, n = banks[product]
            slot_last[place[group_name]] = (bank_full[b], n + 1)

        def features(name, w, src, c0, n, m=P, ready=None):
            bank = take(name)
            k_n = w.shape[1]
            for c in range(n):
                for k in range(k_n):
                    if ready is not None and c == 0 and k % 2 == 0:
                        pe.wait_ge(ev("h_ready"), 4 * ready + k // 2 + 1)
                    mm = pe.matmul(bank[0:m, c * T:(c + 1) * T], w[:, k, c0 + c * P:c0 + c * P + m],
                                   src[:, k, :], start=(k == 0), stop=(k == k_n - 1))
            full(mm, name)

        def tokens(name, w, src, blk, c0, n):
            bank = take(name)
            k_n = w.shape[1]
            for k in range(k_n):
                mm = pe.matmul(bank[:, 0:n], src[:, k, blk * P:(blk + 1) * P], w[:, k, c0:c0 + n],
                               start=(k == 0), stop=(k == k_n - 1))
            full(mm, name)

        def sum_chunks(name, src, ks, lhs):
            bank = take(name)
            for n, cs in enumerate(ks):
                for c in cs:
                    mm = pe.matmul(bank[:, n * T:(n + 1) * T], lhs, src[:, c, :],
                                   start=(c == cs[0]), stop=(c == cs[-1]))
            full(mm, name)

        def head_rows(name, q, qc, k, kc, half):
            bank = take(name)
            r = slice(half * HEAD, half * HEAD + HEAD)
            pe.matmul(bank[:, 0:P], q[r, qc, 0:P], k[r, kc, 0:P], start=True, stop=True)
            mm = pe.matmul(bank[:, P:W3], q[r, qc, P:T], k[r, kc, 0:T], start=True, stop=True)
            full(mm, name)

        def turn_rows(name, src):
            bank = take(name)
            for j in range(3):
                mm = pe.transpose(bank[:, j * P:(j + 1) * P], src[:, j * P:(j + 1) * P], ident[:, :])
            full(mm, name)

        def apply_values(bank, c, v, cols, wT, half=None):
            rows = slice(0, P) if half is None else slice(half * HEAD, half * HEAD + HEAD)
            pe.matmul(bank[rows, c * T:(c + 1) * T], v[:, 0, cols], wT[:, 0:T], start=True, stop=False)
            return pe.matmul(bank[rows, c * T + P:(c + 1) * T], v[:, 1, cols], wT[:, T:W3],
                             start=False, stop=True)

        def norm_sums(tag, centred):
            if centred:
                bank = take(tag + "mean")
                for c in range(KC):
                    if c % 2 == 0:
                        read_out(pe, centred[c // 2])
                    mm = pe.matmul(bank[:, 0:T], ones_d, xT[:, c, :], start=(c == 0), stop=(c == KC - 1))
                full(mm, tag + "mean")
            bank = take(tag + "var")
            for c in range(KC):
                if c % 2 == 0:
                    pe.wait_ge(ev("sq_d"), 4 * norm_sums.n + c // 2 + 1)
                mm = pe.matmul(bank[:, 0:T], ones_d, wide[:, c, :], start=(c == 0), stop=(c == KC - 1))
            full(mm, tag + "var")
            norm_sums.n += 1
        norm_sums.n = 0
        ones_d = means[:, 0, :]

        def head_values(tag, heads, turned_rows, v, v_cols, prob, first_i, product_of, where):
            for i in range(heads + 1):
                if i < heads:
                    turned_rows(i)
                if i >= 1:
                    h = i - 1
                    name = product_of(h)
                    if name not in banks:
                        take(name)
                    read_out(pe, f"{tag}t{h}")
                    c, half = where(h)
                    mm = apply_values(psum[:, banks[name][0], :], c, v, v_cols(h), prob[:, (first_i + h) % 2, :], half)
                    if h == heads - 1 or product_of(h + 1) != name:
                        full(mm, name)
                        b, n = banks[name]
                        values_done[(tag, h)] = (bank_full[b], n + 1)
                    else:
                        mm.then_inc(ev("values"), 1)
                        head_values.n += 1
                        values_done[(tag, h)] = (ev("values"), head_values.n)
        head_values.n = 0

        def project_aside(i):
            g, name = [("z0", "z0"), ("z0", "z1"), ("z1", "z2"), ("z1", "z3"), ("g1", "g2"), ("g1", "g3")][i]
            features(name, weights(g), hT, 256 * (i % 2), 2)
            if i % 2:
                last_of(g, name)

        def ssm_values(h):
            pe.wait_ge(ev("decay"), h + 1)
            name = f"yssm{h // 4}"
            if h % 4 == 0:
                take(name)
            mm = apply_values(psum[:, banks[name][0], :], h // 2 % 2, x_tok, slice(h * HEAD, (h + 1) * HEAD),
                              decay[:, h % 2, :], h % 2)
            if h % 4 == 3:
                full(mm, name)
                b, n = banks[name]
                values_done[("ssm", h)] = (bank_full[b], n + 1)
            else:
                mm.then_inc(ev("values"), 1)
                head_values.n += 1
                values_done[("ssm", h)] = (ev("values"), head_values.n)

        pe.wait_ge(ev("const_in"), 32)
        pe.wait_ge(ev("means_set"), 6)
        pe.wait_ge(ev("x_in"), 16)
        for c in range(0, KC, 2):
            bank = take(f"x{c}")
            for j in range(2):
                for b in range(NB):
                    mm = pe.transpose(bank[:, (j * NB + b) * P:(j * NB + b + 1) * P],
                                      x_in[:, b, (c + j) * P:(c + j + 1) * P], ident[:, :])
            full(mm, f"x{c}")
        norm_sums("in.", [f"x{c}" for c in (0, 2, 4, 6)])
        pe.wait_ge(ev("rows_in"), 16 * (len(row_loads) + 2 * len(twice)))
        bank = take("vecs")
        for t in range(2):
            mm = pe.transpose(bank[:, t * P:t * P + vec_tiles[t]], vec_rows[0:vec_tiles[t], t, :],
                              ident[0:vec_tiles[t], 0:vec_tiles[t]])
        full(mm, "vecs")
        bank = take("bias")
        pe.wait_ge(ev("bcast_in"), 16 * N_BCAST)
        mm = pe.matmul(bank[0:AH, :], rel_bias[:, :], K["hot"][0:32, :], start=True, stop=True)
        full(mm, "bias")

        def ada(n):
            for g in range(ada.g, ada.g + n):
                if g == 0:
                    pe.wait_ge(ev("cond"), 1)
                w = weights(f"ada{g}")
                for i in range(2):
                    for q in range(4):
                        k = 2 * q + i
                        mm = pe.matmul(psum[32 * q:32 * q + 32, BANKS, :], condT[:, k, 32 - g:64 - g], w[:, k, :],
                                       start=(g == 0 and i == 0), stop=(g == 11 and i == 1), skip_group_check=True)
                mm.then_inc(ev("ada"), 1)
                slot_last[place[f"ada{g}"]] = (ev("ada"), g + 1)
            ada.g += n
        ada.g = 0

        for l in range(DEPTH):
            L = f"{l}."
            for g, name in enumerate(("q", "k")):
                w = weights(f"{name}{l}")
                for j in range(2):
                    features(f"{L}{name}{j}", w, hT, 256 * j, 2, ready=l if (g, j) == (0, 0) else None)
                last_of(f"{name}{l}", f"{L}{name}1")
            w = weights(f"va{l}")
            for b in range(NB):
                tokens(f"{L}va{b}", w, hT, b, 0, 512)
            last_of(f"va{l}", f"{L}va1")
            for j in range(4):
                read_out(pe, f"{L}{'qk'[j // 2]}{j % 2}")
                bank = take(f"{L}rot{j}")
                mm = pe.matmul(bank[:, :], K["rot"][:, :],
                               qk_raw[:, 2 * j:2 * j + 2, :], start=True, stop=True)
                full(mm, f"{L}rot{j}")
            w = weights(f"ga{l}")
            for j in range(2):
                features(f"{L}ga{j}", w, hT, 256 * j, 2)
            last_of(f"ga{l}", f"{L}ga1")
            w = weights(f"bqk{l}")
            for j in range(2):
                features(f"{L}bqk{j}", w, hT, 256 * j, 2)
            last_of(f"bqk{l}", f"{L}bqk1")
            w = weights(f"bvfg{l}")
            for b in range(NB):
                tokens(f"{L}bv{b}", w, hT, b, 0, 256 + HB)
            features(f"{L}gb", w, hT, 256 + HB, 2)
            last_of(f"bvfg{l}", f"{L}gb")
            w = weights(f"cqk{l}")
            for j in range(2):
                features(f"{L}cqk{j}", w, hT, 256 * j, 2)
            last_of(f"cqk{l}", f"{L}cqk1")
            w = weights(f"cvg{l}")
            for b in range(NB):
                tokens(f"{L}cv{b}", w, hT, b, 0, 256)
            features(f"{L}gc", w, hT, 256, 2)
            last_of(f"cvg{l}", f"{L}gc")

            pe.wait_ge(ev("rope"), 4 * l + 4)
            for h in range(HA):
                for m in range(2):
                    head_rows(f"{L}s{h}{m}", qk, h, qk, 4 + h, m)
            read_out(pe, f"{L}cqk1")
            for h in range(HC):
                name, r = f"{L}z{h}", slice(h % 2 * HEAD, h % 2 * HEAD + HEAD)
                bank = take(name)
                pe.matmul(bank[:, 0:T], bc_qk[r, 6 + h // 2, 0:P], bc_qk[r, 4 + h // 2, :],
                          start=True, stop=True)
                mm = pe.matmul(bank[:, T:W3], bc_qk[r, 6 + h // 2, P:T], bc_qk[r, 4 + h // 2, P:T],
                               start=True, stop=True)
                full(mm, name)
            ada(3)
            pe.wait_ge(ev("logf"), l + 1)
            bank = take(f"{L}cumq")
            pe.matmul(bank[:, 0:HB], up, logf[:, 0, :], start=True, stop=True)
            pe.matmul(bank[:, HB:2 * HB], ones, logf[:, 0, :], start=True, stop=False)
            mm = pe.matmul(bank[:, HB:2 * HB], up, logf[:, 1, :], start=False, stop=True)
            full(mm, f"{L}cumq")
            for h in range(HB):
                if h % 2 == 0:
                    bank = take(f"{L}cumk{h // 2}")
                c = h % 2 * T
                pe.matmul(bank[:, c:c + T], logf[:, 0, h:h + 1].broadcast_to([P, P]), up_ones[:, :],
                          start=True, stop=False)
                mm = pe.matmul(bank[:, c + P:c + T], logf[:, 1, h:h + 1].broadcast_to([P, P]), up,
                               start=False, stop=True)
                if h % 2:
                    full(mm, f"{L}cumk{h // 2}")
            for h in range(HB):
                head_rows(f"{L}f{h}", bc_qk, h // 2, bc_qk, 2 + h // 2, h % 2)
            pe.wait_ge(ev("log_fail"), l + 1)
            for h in range(HC):
                bank = take(f"{L}after{h}")
                pe.matmul(bank[:, 0:W3], K["down"][:, :], ls[:, h, :], start=True, stop=False)
                mm = pe.matmul(bank[:, P:T], ones, ls[:, h, T:W3], start=False, stop=True)
                full(mm, f"{L}after{h}")
            ada(3)
            def turn_a(h):
                pe.wait_ge(ev("wa"), HA * l + h + 1)
                turn_rows(f"{L}at{h}", sc[:, 2 * h, :])

            def turn_f(h):
                pe.wait_ge(ev("wf"), HB * l + h + 1)
                turn_rows(f"{L}ft{h}", sf[:, h, :])

            head_values(f"{L}a", HA, turn_a, va, lambda h: slice(h * P, (h + 1) * P), probT, 0,
                        lambda h: f"{L}oa{h // 2}", lambda h: (h % 2, None))
            head_values(f"{L}f", HB, turn_f, vbc, lambda h: slice(h * HEAD, (h + 1) * HEAD), probT, HA,
                        lambda h: f"{L}ob", lambda h: (h // 2, h % 2))
            o_bank = take(f"{L}oc")
            pe.wait_ge(ev("wc"), l + 1)
            for h in range(HC):
                mm = apply_values(o_bank, h // 2, vbc, slice(256 + h * HEAD, 256 + (h + 1) * HEAD),
                                  zs[:, h, :], h % 2)
            full(mm, f"{L}oc")
            pe.wait_ge(ev("sq_a"), l + 1)
            for j in range(2):
                bank = take(f"{L}ms{j}")
                mm = pe.matmul(bank[:, :], means[:, 1, :], wide[:, 2 * j:2 * j + 2, :], start=True, stop=True)
                full(mm, f"{L}ms{j}")
            pe.wait_ge(ev("y_ready"), l + 1)
            for j in range(2):
                w = weights(f"out{l}.{j}")
                for i in range(2):
                    features(f"{L}out{2 * j + i}", w, yT, 256 * i, 2)
                last_of(f"out{l}.{j}", f"{L}out{2 * j + 1}")
            norm_sums(L, [f"{L}out{j}" for j in range(4)])

        pe.wait_ge(ev("mod_rows"), 1)
        bank = take("mod")
        for i in range(4):
            mm = pe.matmul(bank[:, 12 * i:12 * i + 12], mod_rows[:, i * P:(i + 1) * P], K["mod_sum"][:, :],
                           start=True, stop=True)
        full(mm, "mod")
        norm_sums("m.", None)
        w = weights("q2")
        for j in range(2):
            features(f"q2.{j}", w, hT, 256 * j, 2, ready=None if j else DEPTH + 1)
        last_of("q2", "q2.1")
        w = weights("kvqi")
        features("kvl", w, hT, 0, 2)
        features("qi0", w, hT, 256, 2)
        last_of("kvqi", "qi0")
        w = weights("qkwi")
        features("qi1", w, hT, 0, 2)
        bank = take("ki")
        for half in range(2):
            for k in range(KC):
                mm = pe.matmul(bank[half * HEAD:(half + 1) * HEAD, 0:T], w[:, k, 256:320], hT[:, k, :],
                               start=(k == 0), stop=(k == KC - 1))
        full(mm, "ki")
        bank = take("wi")
        for b in range(NB):
            for k in range(KC):
                mm = pe.matmul(bank[:, b * AH:(b + 1) * AH], hT[:, k, b * P:(b + 1) * P], w[:, k, 320:328],
                               start=(k == 0), stop=(k == KC - 1))
        full(mm, "wi")
        last_of("qkwi", "wi")
        for j in range(3):
            w = weights(f"x{j}")
            for i in range(2):
                features(f"xbc{2 * j + i}", w, hT, 256 * i, 2)
            last_of(f"x{j}", f"xbc{2 * j + 1}")
        w = weights("dtg")
        bank = take("dt")
        for b in range(NB):
            for k in range(KC):
                mm = pe.matmul(bank[:, b * SH:(b + 1) * SH], hT[:, k, b * P:(b + 1) * P], w[:, k, 0:SH],
                               start=(k == 0), stop=(k == KC - 1))
        full(mm, "dt")
        for i in range(2):
            features(f"g{i}", w, hT, SH + 256 * i, 2)
        last_of("dtg", "g1")
        pe.wait_ge(ev("sq_q"), 1)
        for j in range(2):
            bank = take(f"q2ms{j}")
            mm = pe.matmul(bank[:, :], K["half"][:, :], wide[:, 2 * j:2 * j + 2, :], start=True, stop=True)
            full(mm, f"q2ms{j}")
        pe.wait_ge(ev("sq_kv"), 1)
        sum_chunks("kvms", wide, [range(4, 6)], means[:, 2, :])
        read_out(pe, "ki")
        bank = take("kimean")
        mm = pe.matmul(bank[:, 0:T], K["half"][:, :], ki[:, :], start=True, stop=True)
        full(mm, "kimean")
        pe.wait_ge(ev("sq_ki"), 1)
        bank = take("kivar")
        mm = pe.matmul(bank[:, 0:T], K["half"][:, :], wide[:, 6, :], start=True, stop=True)
        full(mm, "kivar")
        w = weights("kvup")
        pe.wait_ge(ev("kvl"), 2)
        for j in range(2):
            features(f"k2.{j}", w, kvl, 256 * j, 2)
        for b in range(NB):
            tokens(f"v2.{b}", w, kvl, b, 512, 512)
        last_of("kvup", "v2.1")
        pe.wait_ge(ev("ki"), 1)
        for h in range(AH):
            name, r = f"is{h}", slice(h % 2 * HEAD, h % 2 * HEAD + HEAD)
            bank = take(name)
            pe.matmul(bank[:, 0:P], qi[r, h // 2, 0:P], ki[r, 0:P], start=True, stop=True)
            mm = pe.matmul(bank[:, P:W3], qi[r, h // 2, P:T], ki[r, 0:T], start=True, stop=True)
            full(mm, name)
        pe.wait_ge(ev("sq_k"), 1)
        for j in range(2):
            bank = take(f"k2ms{j}")
            mm = pe.matmul(bank[:, :], K["half"][:, :], wide[:, 2 * j:2 * j + 2, :], start=True, stop=True)
            full(mm, f"k2ms{j}")
        pe.wait_ge(ev("dta"), 1)
        bank = take("acum")
        for b in range(NB):
            pe.matmul(bank[:, b * SH:(b + 1) * SH], up, dta[:, b, :], start=True, stop=True)
        mm = pe.matmul(bank[:, 2 * SH:3 * SH], ones, dta[:, 0, :], start=True, stop=True)
        full(mm, "acum")
        pe.wait_ge(ev("xs"), 1)
        for b in range(NB):
            for j in range(2):
                bank = take(f"xt{b}{j}")
                for i in range(4):
                    mm = pe.transpose(bank[:, i * P:(i + 1) * P], xbcs[:, 4 * j + i, b * P:(b + 1) * P], ident[:, :])
                full(mm, f"xt{b}{j}")
        for g in range(2):
            bank = take(f"cb{g}")
            pe.matmul(bank[:, 0:T], xbcs[:, 8 + g, 0:P], xbcs[:, 10 + g, :], start=True, stop=True)
            mm = pe.matmul(bank[:, T:W3], xbcs[:, 8 + g, P:T], xbcs[:, 10 + g, P:T], start=True, stop=True)
            full(mm, f"cb{g}")
        read_out(pe, "xt11")
        for h in range(SH):
            bank = take(f"A{h}")
            for b in range(NB):
                mm = pe.matmul(bank[:, b * P:(b + 1) * P], dta[:, b, h:h + 1].broadcast_to([P, P]), up,
                               start=True, stop=True)
            full(mm, f"A{h}")
            if h % 5 == 2 and h // 5 < 3:
                for i in range(2):
                    project_aside(2 * (h // 5) + i)
            if h >= 1:
                ssm_values(h - 1)
        ssm_values(SH - 1)
        for j in range(1, 3):
            w = weights(f"g{j + 1}")
            for i in range(2):
                features(f"g{2 * j + 2 + i}", w, hT, 256 * i, 2)
            last_of(f"g{j + 1}", f"g{2 * j + 3}")
        pe.wait_ge(ev("sq_y"), 1)
        sum_chunks("yms", wide, [range(4), range(4, 8)], means[:, 3, :])
        pe.wait_ge(ev("qk2"), 2)
        for h in range(AH):
            head_rows(f"t{h}", q2, h // 2, k2, h // 2, h % 2)
        def turn_2(h):
            pe.wait_ge(ev("w2"), h + 1)
            turn_rows(f"2.t{h}", sc2[:, h, :])

        head_values("2.", AH, turn_2, v2, lambda h: slice(h * HEAD, (h + 1) * HEAD), probT2, 0,
                    lambda h: f"o2.{h // 4}", lambda h: (h // 2 % 2, h % 2))
        w = weights("ao")
        read_out(pe, "o2.1")
        for j in range(4):
            features(f"ya{j}", w, q2, 256 * j, 2)
        last_of("ao", "ya3")
        pe.wait_ge(ev("y_ssm"), 1)
        for j in range(2):
            w = weights(f"so{j}")
            for i in range(2):
                features(f"ys{2 * j + i}", w, yS, 256 * i, 2)
            last_of(f"so{j}", f"ys{2 * j + 1}")
        pe.wait_ge(ev("mixed"), 4)
        for j in range(2):
            w = weights(f"wo{j}")
            for i in range(2):
                features(f"wo{2 * j + i}", w, zg, 256 * i, 2)
            last_of(f"wo{j}", f"wo{2 * j + 1}")
        norm_sums("f.", None)

        pe.wait_ge(ev("h_ready"), 4 * (DEPTH + 3))
        bank = take("router")
        for b in range(NB):
            for k in range(KC):
                mm = pe.matmul(bank[:, b * NE:(b + 1) * NE], hT[:, k, b * P:(b + 1) * P], w_router[:, k, :],
                               start=(k == 0), stop=(k == KC - 1))
        full(mm, "router")
        for b in range(NB):
            for j in range(2):
                bank = take(f"ht{b}{j}")
                for i in range(4):
                    mm = pe.transpose(bank[:, i * P:(i + 1) * P], hT[:, 4 * j + i, b * P:(b + 1) * P], ident[:, :])
                full(mm, f"ht{b}{j}")
        pe.wait_ge(ev("chosen"), 1)
        bank = take("pos")
        pe.matmul(bank[:, 0:NE], K["before"][:, :], rt[:, 0, 0, :], start=True, stop=True)
        pe.matmul(bank[:, NE:2 * NE], ones, rt[:, 0, 0, :], start=True, stop=False)
        mm = pe.matmul(bank[:, NE:2 * NE], K["before"][:, :], rt[:, 0, 1, :], start=False, stop=True)
        full(mm, "pos")
        bank = take("count")
        for b in range(NB):
            mm = pe.matmul(bank[0:NE, 0:1], rt[:, 0, b, :], ones[:, 0:1], start=(b == 0), stop=(b == NB - 1))
        full(mm, "count")
        bank = take("gateT")
        for b in range(NB):
            mm = pe.transpose(bank[0:NE, b * P:(b + 1) * P], rt[:, 1, b, :], ident[:, :])
        full(mm, "gateT")
        pe.wait_ge(ev("passes"), 1)
        bank = take("cum_passes")
        mm = pe.matmul(bank[0:NE, 0:1], up_ones[0:NE, 0:NE], passes[:, 1:2], start=True, stop=True)
        full(mm, "cum_passes")
        pe.wait_ge(ev("passes"), 2)
        bank = take("todo")
        M = MAX_EXTRA
        pe.matmul(bank[0:1, 0:M], up_ones[0:NE, P:P + 1], passes[:, 4:4 + M], start=True, stop=True)
        pe.matmul(bank[0:1, M:2 * M], passes[:, 1:2], passes[:, 4:4 + M], start=True, stop=True)
        mm = pe.matmul(bank[0:1, 2 * M:2 * M + 1], passes[:, 1:2], up_ones[0:NE, P:P + 1], start=True, stop=True)
        full(mm, "todo")

        for b in range(BANKS):
            uses = len([1 for x, _ in banks.values() if x == b])
            pe.wait_ge(bank_free[b], uses)
        pe.wait_ge(ev("b_dn_in"), 16)
        pe.wait_ge(ev("zero"), 1)
        for j in range(4):
            pe.matmul(psum[:, j, :], zero[:, :], hT[:, 0:2, :], start=True, stop=False, skip_group_check=True)
        for c in range(KC):
            mm = pe.matmul(psum[:, c // 2, c % 2 * T:(c % 2 + 1) * T], b_dn[:, c * P:(c + 1) * P], gateT[:, :],
                           start=False, stop=False, skip_group_check=True)

        def add_up():
            for i in range(4):
                for half in range(2):
                    c = 4 * half + i
                    r = slice(half * CAP, (half + 1) * CAP)
                    mm = pe.matmul(psum[:, c // 2, c % 2 * T:(c % 2 + 1) * T], o_slot[r, i * P:(i + 1) * P],
                                   putT[r, :], start=False, stop=False, skip_group_check=True)
            mm.then_inc(ev("added"), 1)

        def expert(n, first=False):
            pe.wait_ge(ev("picked"), n + 1)
            for c in range(KC):
                for b in range(NB):
                    mm = pe.matmul(psum[:, 6, c * CAP:(c + 1) * CAP], h_tok[:, b, c * P:(c + 1) * P],
                                   pick[:, b, :], start=(b == 0), stop=(b == NB - 1))
            mm.then_inc(ev("gathered"), 1)
            pe.wait_ge(ev("hg"), n + 1)
            for part in range(2):
                if part and not first:
                    pe.wait_ge(ev("o_slot"), n)
                w = []
                for half in range(2):
                    slot = expert_slot[2 * part + half]
                    pe.wait_ge(slot_full[slot], 16 * (slot_uses[slot] + 1) + 16 * n)
                    w.append(slot_view(slot, KC, 512))
                for k in range(KC):
                    for half in range(2):
                        mm = pe.matmul(psum[half * CAP:(half + 1) * CAP, 4 + part, :], hg[:, k, :],
                                       w[half][:, k, :], start=(k == 0), stop=(k == KC - 1))
                mm.then_inc(ev("gu_done"), 1)
            if not first:
                add_up()
            for b in range(NB):
                mm = pe.transpose(psum[:, 7, b * P:(b + 1) * P],
                                  pick_gate[:, b, :, :].rearrange("p i s -> p (i s)"), ident[:, :])
            mm.then_inc(ev("turned"), 1)
            pe.wait_ge(ev("hidden"), n + 1)
            for i in range(4):
                mm = pe.transpose(psum[:, 6, i * P:(i + 1) * P], hidden[:, 2, i * P:(i + 1) * P], ident[:, :])
            mm.then_inc(ev("hidden_turned"), 1)
            pe.wait_ge(ev("hiddenT"), n + 1)
            pe.wait_ge(ev("putT"), n + 1)
            for half in range(2):
                pe.wait_ge(ev(f"down_in{half}"), 16 * n + 16)
            for k in range(KC):
                for half in range(2):
                    mm = pe.matmul(psum[half * CAP:(half + 1) * CAP, 5, :],
                                   hiddenT[:, k % 4, k // 4 * CAP:(k // 4 + 1) * CAP],
                                   w_down[:, half, k * 512:(k + 1) * 512], start=(k == 0), stop=(k == KC - 1))
            mm.then_inc(ev("down_done"), 1)

        expert(0, True)
        with pe.Fori(1, NE) as e:
            expert(e)
        pe.wait_ge(ev("todo"), 1)
        extra = pe.value_load(todo[0:1, 2 * M:2 * M + 1], min_val=0, max_val=M)
        with pe.Fori(0, M) as i:
            with pe.If(extra > i):
                expert(i + NE)
            pe.nop()
        pe.wait_ge(ev("o_slot"), extra + NE)
        pe.wait_ge(ev("putT"), extra + NE)
        add_up()
        pe.wait_ge(ev("final"), KC)
        for b in range(NB):
            for j in range(2):
                for i in range(4):
                    mm = pe.transpose(psum[:, 4 + 2 * b + j, i * P:(i + 1) * P],
                                      xT[:, 4 * j + i, b * P:(b + 1) * P], ident[:, :])
                mm.then_inc(ev("turned_out"), 1)

    @block.sync
    def _(sp):
        sp.dma_start(x_in[:, :, :], a["x"][0].rearrange("(b p) d -> p b d", p=P)).then_inc(ev("x_in"), 16)
        for pack in (False, True):
            sp.dma_start(const_tiles[pack][:, :], packs[pack][1][:, :]).then_inc(ev("const_in"), 16)
        for g, (name, src) in enumerate(groups):
            slot = g % RING
            if g >= RING:
                sp.wait_ge(*slot_last[g - RING])
            sp.dma_start(slot_view(slot, src.shape[1], src.shape[2]), src).then_inc(slot_full[slot], 16)
            if name == "ada0":
                read_out(sp, "bias")
                sp.dma_start(bias_dram[:, :, :], biasrev[:, :].rearrange("h (o j) -> h o j", o=1)
                             .broadcast_to([AH, P, 2 * T])).then_inc(ev("bias_out"), 16)
            if name == "x0":
                sp.wait_ge(ev("bias_out"), 16)
                sp.wait_ge(ev("h_ready"), 4 * (DEPTH + 1))
                for qb in range(NB):
                    width = (qb + 1) * P
                    src = bass.AP(tensor=bias_dram[:, :, :].tensor, offset=T - 1 - qb * P,
                                  ap=[[2 * T - 1, P], [P * 2 * T, AH], [1, width]])
                    dst = bm[:, :, 0:P] if qb == 0 else bm[:, :, P:W3]
                    sp.dma_start(dst, src).then_inc(ev("bias_in"), 16)

        def gate_up(n, e, peeled=False):
            for j in range(4):
                slot = expert_slot[j]
                if peeled:
                    sp.wait_ge(*slot_last[NG - RING + j])
                else:
                    sp.wait_ge(ev("gu_done"), 2 * n + j // 2 - 1)
                sp.dma_start(slot_view(slot, KC, 512), w_gu[bass.ds(e, 1), :, :, 512 * j:512 * j + 512]
                             .rearrange("e p k n -> (e p) k n")).then_inc(slot_full[slot], 16)

        gate_up(0, 0, True)
        with sp.Fori(1, NE) as e:
            gate_up(e, e)
        sp.wait_ge(ev("todo"), 1)
        extra = sp.value_load(todo[0:1, 2 * MAX_EXTRA:2 * MAX_EXTRA + 1], min_val=0, max_val=MAX_EXTRA)
        with sp.Fori(0, MAX_EXTRA) as i:
            with sp.If(extra > i):
                e = sp.value_load(todo[0:1, bass.ds(i, 1)], min_val=0, max_val=NE - 1)
                gate_up(i + NE, e)
            sp.nop()
        for b in range(NB):
            sp.wait_ge(ev("out_rows"), 2 * b + 2)
            sp.dma_start(out[0, b * P:(b + 1) * P, :], h_tok[:, b, :]).then_inc(ev("out_done"), 16)
        sp.wait_ge(ev("out_done"), 16 * NB)

    @block.gpsimd
    def _(pool):
        b_gu = a["b_gu_2"][0].rearrange("e (g h n) -> h e g n", g=2, h=2)

        def down(n, e, peeled=False):
            if not peeled:
                pool.wait_ge(ev("u_in"), n)
            for half in range(2):
                pool.dma_start(gu_bias[half * CAP:(half + 1) * CAP, :, :],
                               b_gu[half, bass.ds(e, 1), :, :].rearrange("e g n -> (e g) n").partition_broadcast(CAP))\
                    .then_inc(ev("gu_bias_in"), 16)
            if not peeled:
                pool.wait_ge(ev("down_done"), n)
            for half in range(2):
                pool.dma_start(w_down[:, half, :].rearrange("p (k n) -> p k n", k=KC),
                               w_dn[bass.ds(e, 1), :, :, 512 * half:512 * half + 512]
                               .rearrange("e p k n -> (e p) k n")).then_inc(ev(f"down_in{half}"), 16)

        pool.wait_ge(ev("h_ready"), 4 * (DEPTH + 3))
        pool.dma_start(b_dn[:, :], a["b_dn_2"][0]).then_inc(ev("b_dn_in"), 16)
        down(0, 0, True)
        with pool.Fori(1, NE) as e:
            down(e, e)
        pool.wait_ge(ev("todo"), 1)
        extra = pool.value_load(todo[0:1, 2 * MAX_EXTRA:2 * MAX_EXTRA + 1], min_val=0, max_val=MAX_EXTRA)
        with pool.Fori(0, MAX_EXTRA) as i:
            with pool.If(extra > i):
                e = pool.value_load(todo[0:1, bass.ds(i, 1)], min_val=0, max_val=NE - 1)
                down(i + NE, e)
            pool.nop()

    @block.scalar
    def _(act):
        ch = Chain(act, "act_done")

        def f(out_, in_, func, s=None, **kw):
            ch.after(act.activation(out_, in_, func, **kw), s)

        def read(name, out_, func=ACT.Copy, cols=slice(0, 512), rows=slice(0, P), last=True, **kw):
            ins = act.activation(out_, shaped(product(act, name)[rows, cols], out_), func, **kw)
            if last:
                ch.free(ins, name)
            else:
                ch.after(ins)

        for tile, at, n, src in row_loads:
            act.dma_start(vec_rows[at:at + n, tile, :], src).then_inc(ev("rows_in"), 16)
        for at, src in twice:
            for half in range(2):
                act.dma_start(vec_rows[at:at + 1, 1, half * HEAD:(half + 1) * HEAD], src).then_inc(ev("rows_in"), 16)
        alike = [(lam_in[:, i, :], a[n].rearrange("l d -> (l d)")) for i, n in
                 enumerate(("lambda_q1", "lambda_k1", "lambda_q2", "lambda_k2"))]
        alike += [(b_forget[:, :], a["b_forget"].rearrange("l h -> (l h)")), (dt_bias[:, :], a["dt_bias_2"][0]),
                  (a_log[:, :], a["a_log_2"][0]), (b_router[:, :], a["b_router_2"][0])]
        for dst, src in alike:
            act.dma_start(dst, src.partition_broadcast(P)).then_inc(ev("bcast_in"), 16)
        for half in range(2):
            src = a["d_skip_2"][0].rearrange("(c two) -> two c", two=2)[half]
            with nc.allow_non_contiguous_dma(reason="16 numbers"):
                act.dma_start(d_skip[half * HEAD:(half + 1) * HEAD, :], src.partition_broadcast(HEAD))\
                    .then_inc(ev("bcast_in"), 16)
        act.dma_start(rel_bias[:, :], a["rel_bias_2"]).then_inc(ev("bcast_in"), 16)
        act.dma_start(w_router[:, :, :], a["w_router_2"][0].rearrange("(k p) n -> p k n", p=P))\
            .then_inc(ev("bcast_in"), 16)

        norms = [0]

        def rstd(name, out_, eps_col, s=None, cols=slice(0, 512)):
            read(name, out_, ACT.Ln, cols=cols, bias=eps[:, eps_col:eps_col + 1])
            f(out_, out_, ACT.Exp, s, scale=-0.5)

        def exp_table():
            act.preload_act_table_set("natural_log_exp_and_others")

        def norm(tag, centred, scale, shift, dst, e):
            exp_table()
            n = norms[0]
            norms[0] += 1
            for j in range(4):
                r = slice(2 * j, 2 * j + 2)
                if centred is True:
                    act.wait_ge(ev("centred"), 4 * centrings[0] + j + 1)
                elif centred is not None:
                    read_out(act, centred[j])
                act.activation(wide[:, r, :], xT[:, r, :], ACT.Square).then_inc(ev("sq_d"), 1)
            centrings[0] += centred is True
            rstd(tag + "var", stat[:, :], e, ev("rstd"), cols=slice(0, T))
            if tag == "in.":
                read_out(act, "vecs")
            for j in range(4):
                act.wait_ge(ev("scaled"), 4 * n + j + 1)
                for c in (2 * j, 2 * j + 1):
                    ins = act.activation(dst[:, c, :], dst[:, c, :], ACT.Identity, bias=shift(c), scale=scale(c))
                ins.then_inc(ev("h_ready"), 1)
            act.wait_ge(ev("h_ready"), 4 * n + 4)

        centrings = [0]
        act.wait_ge(ev("means_set"), 6)
        norm("in.", True, lambda c: vec("ln_in_g", c), lambda c: vec("ln_in_b", c), hT, 0)
        act.wait_ge(ev("means_set"), 7)
        f(condT[:, :, 32:33], vec("c", 0, 8).rearrange("p (k o) -> p k o", o=1), ACT.Silu, ev("cond"))
        act.wait_ge(ev("lam_sum"), 1)
        f(lam[:, 0:4], lam[:, 0:4], ACT.Exp, ev("lam_exp"))

        for l in range(DEPTH):
            L = f"{l}."
            for j in range(4):
                read(f"{L}{'qk'[j // 2]}{j % 2}", qk_raw[:, 2 * j:2 * j + 2, :])
            for b in range(NB):
                read(f"{L}va{b}", va[:, b, :])
            for j in range(2):
                read(f"{L}ga{j}", gate[:, 2 * j:2 * j + 2, :], ACT.Silu)
            for j in range(2):
                read(f"{L}bqk{j}", bc_qk[:, 2 * j:2 * j + 2, :])
            for b in range(NB):
                read(f"{L}bv{b}", vbc[:, b, 0:256], cols=slice(0, 256), last=False)
                read(f"{L}bv{b}", logf[:, b, :], cols=slice(256, 256 + HB))
            read(f"{L}gb", gate[:, 4:6, :], ACT.Silu)
            for j in range(2):
                read(f"{L}cqk{j}", bc_qk[:, 4 + 2 * j:6 + 2 * j, :])
            for b in range(NB):
                read(f"{L}cv{b}", vbc[:, b, 256:512], cols=slice(0, 256))
            read(f"{L}gc", gate[:, 6:8, :], ACT.Silu)
            exp_table()
            act.wait_ge(ev("forget_x"), l + 1)
            f(small[:, 8:16], small[:, 0:8], ACT.Abs)
            f(small[:, 8:16], small[:, 8:16], ACT.Exp, scale=-1.0)
            f(small[:, 8:16], small[:, 8:16], ACT.Ln, ev("forget_ln"), bias=1.0)
            for h in range(HC):
                read(f"{L}z{h}", zs[:, h, :], cols=slice(0, W3), scale=HEAD ** -0.5)
            f(ls[:, :, :], zs[:, :, :], ACT.Abs)
            f(ls[:, :, :], ls[:, :, :], ACT.Exp, scale=-1.0)
            f(ls[:, :, :], ls[:, :, :], ACT.Ln, ev("c_ln"), bias=1.0)
            act.wait_ge(ev("a_max"), l + 1)
            row_exp(act, sc, 0, 8, row_max, row_sum, 0, 8, ev("a_exp"))
            act.wait_ge(ev("f_max"), l + 1)
            row_exp(act, sf, 0, 4, row_max, row_sum, 16, 20, ev("f_exp"))
            act.wait_ge(ev("c_exponent"), l + 1)
            f(zs[:, :, :], zs[:, :, :], ACT.Exp, ev("wc"))
            for i in range(HA + HB):
                tag, h = ("a", i) if i < HA else ("f", i - HA)
                if i >= 2:
                    before = ("a", i - 2) if i - 2 < HA else ("f", i - 2 - HA)
                    act.wait_ge(*values_done[(L + before[0], before[1])])
                read(f"{L}{tag}t{h}", probT[:, i % 2, :], cols=slice(0, W3))
                if i == 3:
                    read(f"{L}oa0", yT[:, 0:2, :])
                if i == 5:
                    read(f"{L}oa1", yT[:, 2:4, :])
                    f(wide[:, 0:4, :], yT[:, 0:4, :], ACT.Square, ev("sq_a"))
            for j in range(2):
                rstd(f"{L}ms{j}", wide[:, 4 + 2 * j:6 + 2 * j, :], 0, ev("rstd_a"))
            norm(L, True, lambda c: vec("ln_g", 8 * l + c), lambda c: vec("ln_b", 8 * l + c),
                 xT if l == DEPTH - 1 else hT, 0)

        act.wait_ge(ev("mod"), 2)
        norm("m.", None, lambda c: mix_scale[:, c:c + 1], lambda c: modT[:, c:c + 1], hT, 1)
        for j in range(2):
            read(f"q2.{j}", q2[:, 2 * j:2 * j + 2, :])
        f(wide[:, 0:4, :], q2[:, :, :], ACT.Square, ev("sq_q"))
        read("kvl", kvl[:, :, :])
        f(wide[:, 4:6, :], kvl[:, :, :], ACT.Square, ev("sq_kv"))
        for j in range(2):
            read(f"qi{j}", qi[:, 2 * j:2 * j + 2, :], scale=HEAD ** -0.5)
        read("ki", ki[:, :], cols=slice(0, T))
        read("wi", wi[:, :, :], cols=slice(0, 2 * AH), scale=AH ** -0.5)
        for i in range(6):
            read(f"xbc{i}", xbc[:, 2 * i:2 * i + 2, 3:T + 3])
        act.wait_ge(ev("dt_x"), 1)
        f(dtx[:, 1, :], dtx[:, 0, :], ACT.Abs)
        f(dtx[:, 1, :], dtx[:, 1, :], ACT.Exp, ev("dt_u"), scale=-1.0)
        f(exp_a[:, :], a_log[:, :], ACT.Exp)
        act.wait_ge(ev("dt_w"), 1)
        f(dtx[:, 3, :], dtx[:, 2, :], ACT.Ln, ev("dt_ln"))
        for i in range(2):
            read(f"g{i}", ga[:, 2 * i:2 * i + 2, :], ACT.Sigmoid)
        exp_table()
        for j in range(2):
            rstd(f"q2ms{j}", wide[:, 2 * j:2 * j + 2, :], 1, ev("rstd_q"))
        rstd("kvms", stat[:, :], 1, ev("rstd_kv"), cols=slice(0, T))
        act.wait_ge(ev("ki_centred"), 1)
        f(wide[:, 6, :], ki[:, :], ACT.Square, ev("sq_ki"))
        rstd("kivar", wide[:, 7, :], 1, ev("rstd_ki"), cols=slice(0, T))
        for j in range(2):
            read(f"k2.{j}", k2[:, 2 * j:2 * j + 2, :])
        for c in range(12):
            act.wait_ge(ev("conv"), c + 1)
            ins = act.activation(xbcs[:, c, :], xbcs[:, c, :], ACT.Silu, bias=vec("conv_b", c))
        ins.then_inc(ev("xs"), 1)
        act.wait_ge(ev("xs"), 1)
        act.wait_ge(ev("qk2"), 1)
        f(wide[:, 0:4, :], k2[:, :, :], ACT.Square, ev("sq_k"))
        for b in range(NB):
            read(f"v2.{b}", v2[:, b, :])
        for h in range(AH):
            if h >= 2:
                act.wait_ge(ev("index_sum"), h - 1)
            read(f"is{h}", idx[:, 1 + h % 2, :], ACT.Relu, cols=slice(0, W3))
        exp_table()
        for j in range(2):
            rstd(f"k2ms{j}", wide[:, 2 * j:2 * j + 2, :], 1, ev("rstd_k"))
        exp_table()
        for b in range(NB):
            for j in range(2):
                read(f"xt{b}{j}", x_tok[:, b, 512 * j:512 * j + 512])
        for h in range(SH):
            act.wait_ge(ev("decay_exponent"), h + 1)
            f(decay[:, h % 2, :], decay[:, h % 2, :], ACT.Exp, ev("decay_exp"))
            if h % 5 == 2 and h // 5 < 3:
                for i in (2 * (h // 5), 2 * (h // 5) + 1):
                    if i < 4:
                        read(f"z{i}", zg[:, 2 * i:2 * i + 2, :])
                    else:
                        read(f"g{i - 2}", ga[:, 2 * i - 4:2 * i - 2, :])
        f(zg[:, :, :], zg[:, :, :], ACT.Silu, ev("z_gate"))
        f(ga[:, 4:8, :], ga[:, 4:8, :], ACT.Sigmoid, ev("g_late"))
        act.wait_ge(ev("y_gated"), 1)
        f(wide[:, :, :], yS[:, :, :], ACT.Square, ev("sq_y"))
        for i in range(4, 8):
            read(f"g{i}", gs[:, 2 * i - 8:2 * i - 6, :], ACT.Sigmoid)
        exp_table()
        rstd("yms", wide[:, 0:2, :], 1, ev("rstd_y"))
        act.wait_ge(ev("t_max"), 1)
        row_exp(act, sc2, 0, 8, row_max2, row_sum2, 0, 8, ev("t_exp"))
        for h in range(AH):
            if h >= 2:
                act.wait_ge(*values_done[("2.", h - 2)])
            read(f"2.t{h}", probT2[:, h % 2, :], cols=slice(0, W3))
            if h == 5:
                read("o2.0", q2[:, 0:2, :])
        read("o2.1", q2[:, 2:4, :])
        norm("f.", [f"wo{j}" for j in range(4)], lambda c: mix_scale[:, 8 + c:9 + c], lambda c: modT[:, 24 + c:25 + c], hT, 1)

        act.wait_ge(ev("top"), 1)
        for b in range(NB):
            ins = act.activation(rt[:, 5, b, :], rt[:, 2, b, :], ACT.Exp, bias=rsm[:, 20 + b:21 + b])
        ins.then_inc(ev("gate_exp"), 1)
        for b in range(NB):
            for j in range(2):
                read(f"ht{b}{j}", h_tok[:, b, 512 * j:512 * j + 512])

        def expert(n, first=False):
            act.wait_ge(ev("gathered"), n + 1)
            act.activation(hg[:, :, :], psum[:, 6, :].rearrange("p (k s) -> p k s", k=KC), ACT.Copy)\
                .then_inc(ev("hg"), 1)
            act.wait_ge(ev("g_in"), n + 1)
            act.activation(hidden[:, 0, :], gu[:, 0, :], ACT.Sigmoid, scale=1.702).then_inc(ev("g_sig"), 1)
            act.wait_ge(ev("turned"), n + 1)
            act.activation(putT[:, :], psum[:, 7, 0:T], ACT.Copy).then_inc(ev("putT"), 1)
            act.wait_ge(ev("hidden_turned"), n + 1)
            act.activation(hiddenT[:, :, :], psum[:, 6, :].rearrange("p (i s) -> p i s", i=4), ACT.Copy)\
                .then_inc(ev("hiddenT"), 1)
            act.wait_ge(ev("down_done"), n + 1)
            act.activation(o_slot[:, :], psum[:, 5, :], ACT.Copy).then_inc(ev("o_slot"), 1)

        expert(0, True)
        with act.Fori(1, NE) as e:
            expert(e)
        act.wait_ge(ev("todo"), 1)
        extra = act.value_load(todo[0:1, 2 * MAX_EXTRA:2 * MAX_EXTRA + 1], min_val=0, max_val=MAX_EXTRA)
        with act.Fori(0, MAX_EXTRA) as i:
            with act.If(extra > i):
                expert(i + NE)
            act.nop()
        for b in range(NB):
            for j in range(2):
                act.wait_ge(ev("turned_out"), 2 * b + j + 1)
                act.activation(h_tok[:, b, 512 * j:512 * j + 512], psum[:, 4 + 2 * b + j, :], ACT.Copy)\
                    .then_inc(ev("out_rows"), 1)

    @block.vector
    def _(dve):
        ch = Chain(dve, "dve_done")

        def tt(out_, x, y, op, s=None):
            ch.after(dve.tensor_tensor(out_, x, y, op), s)

        def ts(out_, x, s1, s2, op0, op1=None, s=None, **kw):
            ins = dve.tensor_scalar(out_, x, s1, s2, op0, op1, **kw) if op1 is not None else \
                dve.tensor_scalar(out_, x, s1, None, op0, **kw)
            ch.after(ins, s)

        def stt(out_, x, scalar, y, op0, op1, s=None, **kw):
            ch.after(dve.scalar_tensor_tensor(out_, x, scalar, y, op0, op1, **kw), s)

        def over(v, n):
            return v.rearrange("p (o m) -> p o m", o=1).broadcast_to([v.shape[0], n, v.shape[1]])

        two = lambda v: v.rearrange("p (c t) -> p c t", c=2)

        for i, n in enumerate((D, P, 256, 512)):
            ch.after(dve.memset(means[:, i, :], 1.0 / n), ev("means_set"))
        ch.after(dve.memset(eps[:, 0:1], LN_EPS), ev("means_set"))
        ch.after(dve.memset(eps[:, 1:2], RMS_EPS), ev("means_set"))
        ch.after(dve.memset(condT[:, :, :], 0.0), ev("means_set"))
        for c in range(0, KC, 2):
            ch.free(dve.tensor_copy(xT[:, c:c + 2, :], two(product(dve, f"x{c}"))), f"x{c}")
        norms = [0]

        def norm(tag, centred, dst):
            if centred:
                mean = product(dve, tag + "mean")[:, 0:T]
                for j in range(4):
                    r = slice(2 * j, 2 * j + 2)
                    dve.tensor_tensor(xT[:, r, :], xT[:, r, :], over(mean, 2), ALU.subtract)\
                        .then_inc(ev("centred"), 1)
                ch.free(dve.tensor_copy(sink[:, :], mean[:, 0:1]), tag + "mean")
            norms[0] += 1
            dve.wait_ge(ev("rstd"), norms[0])
            for j in range(4):
                r = slice(2 * j, 2 * j + 2)
                dve.tensor_tensor(dst[:, r, :], xT[:, r, :], over(stat[:, :], 2), ALU.mult).then_inc(ev("scaled"), 1)

        norm("in.", True, hT)
        bank = product(dve, "vecs")
        ch.after(dve.tensor_copy(vecs[:, 0, 0:vec_tiles[0]], bank[:, 0:vec_tiles[0]]))
        ch.free(dve.tensor_copy(vecs[:, 1, 0:vec_tiles[1]], bank[:, P:P + vec_tiles[1]]), "vecs")
        ch.free(dve.tensor_copy(biasrev[:, :], product(dve, "bias")[0:AH, :]), "bias")
        dve.wait_ge(ev("bcast_in"), 16 * N_BCAST)
        for l in range(DEPTH):
            for i in range(2):
                r = slice(l * HEAD, (l + 1) * HEAD)
                last = l == DEPTH - 1 and i == 1
                stt(small[:, :], lam_in[:, 2 * i, r], 1.0, lam_in[:, 2 * i + 1, r], ALU.mult, ALU.mult,
                    ev("lam_sum") if last else None, accum_out=lam[:, 2 * l + i:2 * l + i + 1])
        dve.wait_ge(ev("lam_exp"), 1)
        for l in range(DEPTH):
            start = layer_lambda(l)
            stt(lam[:, 4 + l:5 + l], lam[:, 2 * l + 1:2 * l + 2], -start, lam[:, 2 * l:2 * l + 1],
                ALU.add, ALU.subtract)
            ts(lam[:, 6 + l:7 + l], vec("subln_g", l), 1.0 - start, None, ALU.mult)

        def maxima(src, n, cols, c0, c1, s):
            ch.after(dve.tensor_reduce(cols[:, c0:c0 + n], src[:, 0:n, 0:P], AX_X, ALU.max))
            ch.after(dve.tensor_reduce(cols[:, c1:c1 + n], src[:, 0:n, P:W3], AX_X, ALU.max))
            ts(cols[:, c0:c1 + n], cols[:, c0:c1 + n], -1.0, None, ALU.mult, s=s)

        PARTS = ((slice(0, P), 0), (slice(P, W3), 1))

        for l in range(DEPTH):
            L = f"{l}."
            for j in range(4):
                rot = product(dve, f"{L}rot{j}")
                ch.free(dve.tensor_tensor(wide[:, 0:2, :], two(rot), over(K["sin"][:, :], 2), ALU.mult), f"{L}rot{j}")
                tt(qk[:, 2 * j:2 * j + 2, :], qk_raw[:, 2 * j:2 * j + 2, :], over(K["cos"][:, :], 2), ALU.mult)
                tt(qk[:, 2 * j:2 * j + 2, :], qk[:, 2 * j:2 * j + 2, :], wide[:, 0:2, :], ALU.add, ev("rope"))
            read_out(dve, f"{L}bv1")
            tt(small[:, 0:8].rearrange("p (b h) -> p b h", b=NB), logf[:, :, :],
               over(b_forget[:, l * HB:(l + 1) * HB], NB), ALU.add, ev("forget_x"))
            dve.wait_ge(ev("forget_ln"), l + 1)
            stt(logf[:, :, :].rearrange("p b h -> p (b h)"), small[:, 0:8], 0.0, small[:, 8:16],
                ALU.min, ALU.subtract, ev("logf"))
            for i in range(2 * HA):
                name = f"{L}s{i // 2}{i % 2}"
                ch.free(dve.scalar_tensor_tensor(sc[:, i, :], product(dve, name)[:, 0:W3], HEAD ** -0.5,
                                                 K["row_mask"][:, :], ALU.mult, ALU.add), name)
            maxima(sc, 8, row_max, 0, 8, ev("a_max"))
            dve.wait_ge(ev("c_ln"), l + 1)
            stt(flat(ls), flat(zs), 0.0, flat(ls), ALU.max, ALU.add)
            tt(ls[:, :, :], ls[:, :, :], over(K["strict_neg"][:, :], 4), ALU.mult, ev("log_fail"))
            ch.free(dve.tensor_copy(cumq[:, :], product(dve, f"{L}cumq")[:, 0:NB * HB]), f"{L}cumq")
            for h in range(HB):
                name = f"{L}cumk{h // 2}"
                cum = product(dve, name)[:, h % 2 * T:(h % 2 + 1) * T]
                ts(sf[:, h, 0:P], cum[:, 0:P], -1.0, cumq[:, h:h + 1], ALU.mult, ALU.add)
                ins = dve.tensor_scalar(sf[:, h, P:W3], cum, -1.0, cumq[:, HB + h:HB + h + 1], ALU.mult, ALU.add)
                if h % 2:
                    ch.free(ins, name)
                else:
                    ch.after(ins)
            tt(sf[:, :, :], sf[:, :, :], over(K["row_mask"][:, :], HB), ALU.add)
            for h in range(HB):
                name = f"{L}f{h}"
                ch.free(dve.scalar_tensor_tensor(sf[:, h, :], product(dve, name)[:, 0:W3], HEAD ** -0.5,
                                                 sf[:, h, :], ALU.mult, ALU.add), name)
            maxima(sf, 4, row_max, 16, 20, ev("f_max"))
            for h in range(HC):
                name = f"{L}after{h}"
                ch.free(dve.tensor_tensor(zs[:, h, :], product(dve, name)[:, 0:W3], zs[:, h, :], ALU.add), name)
            tt(zs[:, :, :], zs[:, :, :], over(K["strict_add"][:, :], 4), ALU.add, ev("c_exponent"))
            dve.wait_ge(ev("a_exp"), l + 1)
            ch.after(dve.reciprocal(small[:, 16:32], row_sum[:, 0:16]))
            ts(small[:, 32:48], small[:, 16:32], lam[:, 4 + l:5 + l], None, ALU.mult)
            for h in range(HA):
                for cols, q in PARTS:
                    r1, r2 = 16 + 8 * q + 2 * h, 32 + 8 * q + 2 * h + 1
                    ts(sc[:, 2 * h + 1, cols], sc[:, 2 * h + 1, cols], small[:, r2:r2 + 1], None, ALU.mult)
                    stt(sc[:, 2 * h, cols], sc[:, 2 * h, cols], small[:, r1:r1 + 1], sc[:, 2 * h + 1, cols],
                        ALU.mult, ALU.add, ev("wa") if q else None)
            dve.wait_ge(ev("f_exp"), l + 1)
            ch.after(dve.reciprocal(row_sum[:, 16:24], row_sum[:, 16:24]))
            for h in range(HB):
                for cols, q in PARTS:
                    ts(sf[:, h, cols], sf[:, h, cols], row_sum[:, 16 + 4 * q + h:17 + 4 * q + h], None, ALU.mult,
                       s=ev("wf") if q else None)
            for name, c in (("ob", 4), ("oc", 6)):
                ch.free(dve.tensor_tensor(yT[:, c:c + 2, :], two(product(dve, L + name)), gate[:, c:c + 2, :],
                                          ALU.mult), L + name)
            dve.wait_ge(ev("rstd_a"), 2 * l + 2)
            stt(flat(yT[:, 0:4, :]), flat(yT[:, 0:4, :]), lam[:, 6 + l:7 + l], flat(wide[:, 4:8, :]), ALU.mult, ALU.mult)
            tt(yT[:, 0:4, :], yT[:, 0:4, :], gate[:, 0:4, :], ALU.mult, ev("y_ready"))
            for j in range(4):
                name = f"{L}out{j}"
                ch.free(dve.scalar_tensor_tensor(flat(xT[:, 2 * j:2 * j + 2, :]), flat(hT[:, 2 * j:2 * j + 2, :]),
                                                 alpha, product(dve, name), ALU.mult, ALU.add), name)
            norm(L, True, xT if l == DEPTH - 1 else hT)

        dve.wait_ge(ev("ada"), 12)
        ch.after(dve.tensor_copy(mod_rows[:, :], psum[:, BANKS, :]), ev("mod_rows"))
        ch.free(dve.tensor_tensor(modT[:, :].rearrange("p (g i) -> p i g", i=4),
                                  product(dve, "mod")[:, 0:48].rearrange("p (i g) -> p i g", i=4),
                                  vec("b_ada", 0, 48).rearrange("p (g i) -> p i g", i=4), ALU.add), "mod")
        for i, (norm_name, at) in enumerate((("norm_mix", 8), ("norm_ffn", 32))):
            stt(mix_scale[:, 8 * i:8 * i + 8], modT[:, at:at + 8], 1.0, vec(norm_name, 0, 8), ALU.add, ALU.mult,
                ev("mod"))
        norm("m.", False, hT)
        ch.after(dve.memset(xbc[:, :, 0:3], 0.0))
        ch.free(dve.tensor_tensor(dtx[:, 0, :].rearrange("p (b h) -> p b h", b=NB),
                                  product(dve, "dt")[:, 0:2 * SH].rearrange("p (b h) -> p b h", b=NB),
                                  over(dt_bias[:, :], NB), ALU.add), "dt")
        ts(dt2(dt), dtx[:, 0, :], 0.0, None, ALU.max, s=ev("dt_x"))
        dve.wait_ge(ev("dt_u"), 1)
        ts(dtx[:, 2, :], dtx[:, 1, :], 1.0, None, ALU.add, s=ev("dt_w"))
        stt(dtx[:, 0, :], dtx[:, 2, :], -1.0, dtx[:, 1, :], ALU.add, ALU.subtract)
        dve.wait_ge(ev("dt_ln"), 1)
        tt(dt2(dt), dt2(dt), dtx[:, 3, :], ALU.add)
        ch.after(dve.reciprocal(dtx[:, 3, :], dtx[:, 2, :]))
        tt(dtx[:, 0, :], dtx[:, 0, :], dtx[:, 3, :], ALU.mult)
        tt(dt2(dt), dt2(dt), dtx[:, 0, :], ALU.subtract)
        stt_neg = dve.scalar_tensor_tensor(dta[:, :, :], dt[:, :, :], -1.0, over(exp_a[:, :], NB), ALU.mult, ALU.mult)
        ch.after(stt_neg, ev("dta"))
        dve.wait_ge(ev("rstd_q"), 2)
        stt(flat(q2), flat(q2), vec("q_norm_2"), flat(wide[:, 0:4, :]), ALU.mult, ALU.mult, ev("qk2"))
        ch.free(dve.tensor_tensor(ki[:, :], ki[:, :], product(dve, "kimean")[:, 0:T], ALU.subtract), "kimean")
        ch.after(dve.tensor_copy(sink[:, :], ki[:, 0:1]), ev("ki_centred"))
        dve.wait_ge(ev("rstd_kv"), 1)
        for c in range(2):
            stt(kvl[:, c, :], kvl[:, c, :], vec("kv_norm", c), stat[:, :], ALU.mult, ALU.mult, ev("kvl"))
        dve.wait_ge(ev("rstd_ki"), 1)
        tt(ki[:, :], ki[:, :], wide[:, 7, :], ALU.mult)
        ts(ki[:, :], ki[:, :], vec("idx_k_ln_w_2"), vec("idx_k_ln_b_2"), ALU.mult, ALU.add, s=ev("ki"))
        read_out(dve, "xbc5")
        for k in range(4):
            for c in range(12):
                x = xbc[:, c, k:k + T]
                if k == 0:
                    ins = dve.tensor_scalar(xbcs[:, c, :], x, vec("conv_w", c), None, ALU.mult)
                else:
                    dve.wait_ge(ev("tap"), 12 * k - 11 + c)
                    ins = dve.scalar_tensor_tensor(xbcs[:, c, :], x, vec("conv_w", 12 * k + c), xbcs[:, c, :],
                                                   ALU.mult, ALU.add)
                ins.then_inc(ev("conv") if k == 3 else ev("tap"), 1)
        for h in range(AH):
            read_out(dve, f"is{h}")
            for cols, q in PARTS:
                r, w = idx[:, 1 + h % 2, cols], wi[:, q, h:h + 1]
                s = ev("index_sum") if q else None
                if h == 0:
                    ts(idx[:, 0, cols], r, w, None, ALU.mult, s=s)
                else:
                    stt(idx[:, 0, cols], r, w, idx[:, 0, cols], ALU.mult, ALU.add, s)
        dve.wait_ge(ev("rstd_k"), 2)
        stt(flat(k2), flat(k2), vec("k_norm_2"), flat(wide[:, 0:4, :]), ALU.mult, ALU.mult, ev("qk2"))
        sums = product(dve, "acum")
        ts(neg_acum[:, 0:2, :].rearrange("p b h -> p (b h)"), sums[:, 0:2 * SH], -1.0, None, ALU.mult)
        ch.free(dve.tensor_tensor(neg_acum[:, 2, :], sums[:, 2 * SH:3 * SH], neg_acum[:, 0, :], ALU.add), "acum")

        for g in range(2):
            ch.free(dve.tensor_copy(cbs[:, g, :], product(dve, f"cb{g}")[:, 0:W3]), f"cb{g}")

        def decay_in(h):
            A, d = product(dve, f"A{h}"), decay[:, h % 2, :]
            if h >= 2:
                dve.wait_ge(*values_done[("ssm", h - 2)])
            col = K["col_mask"][:, 0:P]
            stt(d[:, 0:P], A[:, 0:P], neg_acum[:, 0, h:h + 1], col, ALU.add, ALU.add)
            ts(d[:, P:T], A[:, P:T], neg_acum[:, 2, h:h + 1], None, ALU.add)
            ch.free(dve.scalar_tensor_tensor(d[:, T:W3], A[:, P:T], neg_acum[:, 1, h:h + 1], col, ALU.add, ALU.add),
                    f"A{h}")
            ch.after(dve.tensor_copy(sink[:, :], d[:, 0:1]), ev("decay_exponent"))

        def decay_out(h):
            d, cb = decay[:, h % 2, :], cbs[:, h // 8, :]
            dve.wait_ge(ev("decay_exp"), h + 1)
            stt(d[:, 0:T], d[:, 0:T], dt[:, 0, h:h + 1], cb[:, 0:T], ALU.mult, ALU.mult)
            stt(d[:, T:W3], d[:, T:W3], dt[:, 1, h:h + 1], cb[:, T:W3], ALU.mult, ALU.mult, ev("decay"))
            if h % 4 == 3:
                name = f"yssm{h // 4}"
                y = product(dve, name)
                for i in range(2):
                    c = h // 4 * 2 + i
                    ins = dve.scalar_tensor_tensor(yS[:, c, :], xbcs[:, c, :], d_skip[:, c:c + 1],
                                                   y[:, i * T:(i + 1) * T], ALU.mult, ALU.add)
                    if i:
                        ch.free(ins, name)
                    else:
                        ch.after(ins)

        for h in range(SH + 1):
            if h < SH:
                decay_in(h)
            if h >= 1:
                decay_out(h - 1)
        dve.wait_ge(ev("z_gate"), 1)
        tt(yS[:, :, :], yS[:, :, :], zg[:, :, :], ALU.mult, ev("y_gated"))

        def top_sum(scores, work, gt, eq, kth, count, need, k):
            ts(gt, scores, kth, 0.0, ALU.is_gt, ALU.add, accum_out=count)
            ts(eq, scores, kth, None, ALU.is_equal)
            ch.after(dve.tensor_tensor_scan(work, eq, eq, 0.0, ALU.add, ALU.max))
            ts(need, count, -1.0, float(k), ALU.mult, ALU.add)
            stt(work, work, need, eq, ALU.is_le, ALU.mult)
            tt(work, work, gt, ALU.add)

        tt(idx[:, 0, :], idx[:, 0, :], K["row_mask"][:, :], ALU.add)
        ch.after(dve.tensor_copy(idx[:, 1, :], idx[:, 0, :]))
        for cols, q in PARTS:
            work, best = idx[:, 1, cols], top8[:, q, :]
            for r in range(TOPK // 8):
                ch.after(dve.max(best, work))
                if r < TOPK // 8 - 1:
                    ch.after(dve.match_replace(work, best, work, -3e38))
            top_sum(idx[:, 0, cols], work, idx[:, 2, cols], idx[:, 3, cols], best[:, 7:8],
                    sm[:, q:q + 1], sm[:, 2 + q:3 + q], TOPK)
        ts(idx[:, 1, :], idx[:, 1, :], -1.0, BIG, ALU.add, ALU.mult)
        tt(idx[:, 0, :], idx[:, 1, :], K["row_mask"][:, :], ALU.add)
        dve.wait_ge(ev("bias_in"), 32)
        tt(bm[:, :, :], bm[:, :, :], over(idx[:, 0, :], AH), ALU.add)

        dve.wait_ge(ev("rstd_y"), 1)
        for c in range(KC):
            stt(yS[:, c, :], yS[:, c, :], vec("ssm_norm", c), wide[:, c // 4, :], ALU.mult, ALU.mult,
                ev("y_ssm") if c == KC - 1 else None)
        for h in range(AH):
            name = f"t{h}"
            ch.free(dve.scalar_tensor_tensor(sc2[:, h, :], product(dve, name)[:, 0:W3], HEAD ** -0.5, bm[:, h, :],
                                             ALU.mult, ALU.add), name)
        maxima(sc2, 8, row_max2, 0, 8, ev("t_max"))
        dve.wait_ge(ev("t_exp"), 1)
        ch.after(dve.reciprocal(row_sum2[:, :], row_sum2[:, :]))
        for h in range(AH):
            for cols, q in PARTS:
                ts(sc2[:, h, cols], sc2[:, h, cols], row_sum2[:, 8 * q + h:8 * q + h + 1], None, ALU.mult,
                   s=ev("w2") if q else None)
        for j in range(4):
            r = slice(2 * j, 2 * j + 2)
            if j == 0:
                dve.wait_ge(ev("g_late"), 1)
            ch.free(dve.tensor_tensor(ga[:, r, :], two(product(dve, f"ya{j}")), ga[:, r, :], ALU.mult), f"ya{j}")
        read_out(dve, "g7")
        for j in range(4):
            r = slice(2 * j, 2 * j + 2)
            ch.free(dve.tensor_tensor(gs[:, r, :], two(product(dve, f"ys{j}")), gs[:, r, :], ALU.mult), f"ys{j}")
            tt(zg[:, r, :], ga[:, r, :], gs[:, r, :], ALU.add, ev("mixed"))
        for j in range(4):
            name = f"wo{j}"
            bank = product(dve, name)
            for i in range(2):
                c = 2 * j + i
                ins = dve.scalar_tensor_tensor(xT[:, c, :], bank[:, i * T:(i + 1) * T], modT[:, 16 + c:17 + c],
                                               xT[:, c, :], ALU.mult, ALU.add)
                if i:
                    ch.free(ins, name)
                else:
                    ch.after(ins)
        norm("f.", False, hT)

        both = lambda v: v.rearrange("p (b e) -> p b e", b=NB)
        ch.after(dve.memset(zero[:, :], 0.0), ev("zero"))
        ch.free(dve.tensor_tensor(rt[:, 2, :, :], both(product(dve, "router")[:, 0:NB * NE]), over(b_router[:, :], NB),
                                  ALU.add), "router")
        for b in range(NB):
            best = rsm[:, 8 * b:8 * b + 8]
            ch.after(dve.max(best, rt[:, 2, b, :]))
            ts(rsm[:, 20 + b:21 + b], best[:, 0:1], -1.0, None, ALU.mult, s=ev("top") if b else None)
        for b in range(NB):
            top_sum(rt[:, 2, b, :], rt[:, 0, b, :], rt[:, 3, b, :], rt[:, 4, b, :],
                    rsm[:, 8 * b + TOPE - 1:8 * b + TOPE], rsm[:, 16 + b:17 + b], rsm[:, 18 + b:19 + b], TOPE)
        dve.wait_ge(ev("gate_exp"), 1)
        for b in range(NB):
            stt(rt[:, 5, b, :], rt[:, 5, b, :], 1.0, rt[:, 0, b, :], ALU.mult, ALU.mult,
                accum_out=rsm[:, 22 + b:23 + b])
        ch.after(dve.reciprocal(rsm[:, 24:26], rsm[:, 22:24]))
        for b in range(NB):
            ts(rt[:, 1, b, :], rt[:, 5, b, :], rsm[:, 24 + b:25 + b], None, ALU.mult, s=ev("chosen") if b else None)
        ch.free(dve.scalar_tensor_tensor(rt[:, 3, :, :], both(product(dve, "pos")[:, 0:NB * NE]), 1.0, rt[:, 0, :, :],
                                         ALU.add, ALU.mult), "pos")
        for r in range(4):
            ts(pos[:, :, r, :], rt[:, 3, :, :], -1.0 - CAP * r, None, ALU.add)
        ch.free(dve.tensor_copy(passes[:, 0:1], product(dve, "count")[0:NE, 0:1]), "count")
        ts(passes[:, 1:2], passes[:, 0:1], CAP + 0.5, None, ALU.is_gt)
        stt(passes[:, 1:2], passes[:, 0:1], 2 * CAP + 0.5, passes[:, 1:2], ALU.is_gt, ALU.add)
        stt(passes[:, 1:2], passes[:, 0:1], 3 * CAP + 0.5, passes[:, 1:2], ALU.is_gt, ALU.add, ev("passes"))
        ch.free(dve.tensor_copy(gateT[:, :], product(dve, "gateT")[0:NE, 0:T]), "gateT")
        ch.free(dve.tensor_copy(passes[:, 2:3], product(dve, "cum_passes")[0:NE, 0:1]), "cum_passes")
        M = MAX_EXTRA
        ts(passes[:, 4:4 + M], K["iota"][0:NE, 0:M], passes[:, 2:3], None, ALU.is_ge, s=ev("passes"))
        bank = product(dve, "todo")
        ch.free(dve.tensor_copy(todo_f[:, 0:2 * M + 1], bank[0:1, 0:2 * M + 1]), "todo")
        stt(todo_f[:, M:2 * M], K["iota"][0:1, 1:M + 1], float(1), todo_f[:, M:2 * M], ALU.mult, ALU.subtract)
        stt(todo_f[:, M:2 * M], todo_f[:, M:2 * M], float(NE), todo_f[:, 0:M], ALU.mult, ALU.add)
        ch.after(dve.tensor_copy(todo[:, 0:2 * M + 1], todo_f[:, 0:2 * M + 1]), ev("todo"))

        pos_at = pos[:, :, :, :].rearrange("p b r e -> p b (r e)")

        def expert(n, e, col, first=False):
            if not first:
                dve.wait_ge(ev("turned"), n)
            for b in range(NB):
                where = pos_at[:, b, bass.ds(col, 1)]
                dve.tensor_scalar(pick[:, b, :], K["iota"][:, :], where, None, ALU.is_equal)
                ins = dve.tensor_scalar(pick_gate[:, b, :, :], over(K["iota"][:, :], 2), where,
                                        rt[:, 1, b, bass.ds(e, 1)], ALU.is_equal, ALU.mult)
            ins.then_inc(ev("picked"), 1)
            dve.wait_ge(ev("gu_bias_in"), 32 * n + 32)
            for part in range(2):
                v = gu[:, part, :]
                dve.wait_ge(ev("gu_done"), 2 * n + part + 1)
                dve.tensor_tensor(v, psum[:, 4 + part, :], gu_bias[:, part, :], ALU.add).then_inc(ev("gu_in"), 1)
                dve.wait_ge(ev("gu_in"), 2 * n + part + 1)
                if part == 0:
                    dve.tensor_scalar(v, v, 7.0, None, ALU.min).then_inc(ev("g_in"), 1)
                else:
                    dve.tensor_scalar(v, v, 7.0, -7.0, ALU.min, ALU.max).then_inc(ev("u_in"), 1)
            dve.wait_ge(ev("u_in"), n + 1)
            dve.scalar_tensor_tensor(hidden[:, 1, :], gu[:, 1, :], 1.0, gu[:, 0, :], ALU.add, ALU.mult)\
                .then_inc(ev("ug"), 1)
            dve.wait_ge(ev("ug"), n + 1)
            dve.wait_ge(ev("g_sig"), n + 1)
            dve.tensor_tensor(hidden[:, 2, :], hidden[:, 1, :], hidden[:, 0, :], ALU.mult).then_inc(ev("hidden"), 1)

        expert(0, 0, 0, True)
        with dve.Fori(1, NE) as e:
            expert(e, e, e)
        extra = dve.value_load(todo[0:1, 2 * M:2 * M + 1], min_val=0, max_val=M)
        with dve.Fori(0, M) as i:
            with dve.If(extra > i):
                e = dve.value_load(todo[0:1, bass.ds(i, 1)], min_val=0, max_val=NE - 1)
                col = dve.value_load(todo[0:1, bass.ds(i + M, 1)], min_val=0, max_val=4 * NE - 1)
                expert(i + NE, e, col)
            dve.nop()
        dve.wait_ge(ev("added"), extra + NE)
        for c in range(KC):
            stt(xT[:, c, :], psum[:, c // 2, c % 2 * T:(c % 2 + 1) * T], modT[:, 40 + c:41 + c], xT[:, c, :],
                ALU.mult, ALU.add, ev("final"))

    ctx.close()


_INS = ["x", "ln_in_g", "ln_in_b", "w_in", "b_forget", "lambda_q1", "lambda_k1", "lambda_q2", "lambda_k2", "subln_g",
        "w_out", "ln_g", "ln_b", "c_2", "rel_bias_2", "w_ada_2", "b_ada_2", "norm_mix_2", "norm_ffn_2", "w_in_2",
        "kv_norm_2", "w_kv_up_2", "q_norm_2", "k_norm_2", "idx_k_ln_w_2", "idx_k_ln_b_2", "w_attn_o_2", "conv_w_2",
        "conv_b_2", "dt_bias_2", "a_log_2", "d_skip_2", "ssm_norm_2", "w_ssm_o_2", "w_out_2", "w_router_2",
        "b_router_2", "w_gu_2", "b_gu_2", "w_dn_2", "b_dn_2"]


def kernel(**inputs):
    import numpy as _np
    import concourse.bacc as _bacc
    from concourse import mybir as _mybir
    from concourse.bass_utils import run_bass_kernel_spmd as _run

    nc = _bacc.Bacc("TRN2", target_bir_lowering=False, num_devices=1)
    arrays, aps = {}, {}
    for name in _INS:
        arr = _np.ascontiguousarray(inputs[name])
        arrays[f"in_{name}"] = arr
        aps[name] = nc.dram_tensor(f"in_{name}", arr.shape, _mybir.dt.from_np(arr.dtype), kind="ExternalInput").ap()
    out = nc.dram_tensor("out", inputs["x"].shape, _mybir.dt.float32, kind="ExternalOutput").ap()
    mixer_moe_kernel(nc, aps, out)
    r = _run(nc, [arrays], core_ids=[0])
    return r.results[0]["out"]
```
